# Optimizing a Trainium2 kernel written in Bass

```python
import jax, jax.numpy as jnp
from jax import lax
import numpy as np

D_MODEL = 4096
BATCH = 1
SEQ = 256
DEPTH = 1

MIX_WIDTH = D_MODEL
SB_WIDTH = MIX_WIDTH // 2
CONV_WIDTH = MIX_WIDTH - SB_WIDTH
HEAD_DIM = 128
SB_HEADS = SB_WIDTH // HEAD_DIM
CONV_KERNEL = 31
Q_BLOCK = 128
EPS = 1e-6
IN_COLS = 4 * SB_WIDTH + 3 * CONV_WIDTH

kernel_name = "hybrid_stickbreak_conformer_adaln"

def rms_norm(x, g):
    x32 = x.astype(jnp.float32)
    y = x32 * lax.rsqrt(jnp.mean(x32 * x32, axis=-1, keepdims=True) + EPS)
    return (y * g.astype(jnp.float32)).astype(x.dtype)

def layer_norm(x, g, b):
    x32 = x.astype(jnp.float32)
    mu = jnp.mean(x32, axis=-1, keepdims=True)
    xc = x32 - mu
    var = jnp.mean(xc * xc, axis=-1, keepdims=True)
    y = xc * lax.rsqrt(var + EPS) * g.astype(jnp.float32) + b.astype(jnp.float32)
    return y.astype(x.dtype)

def stick_breaking_attention(q, k, v):
    B, H, S, Dh = q.shape
    nb = S // Q_BLOCK
    scale = Dh ** -0.5
    q_blocks = q.reshape(B, H, nb, Q_BLOCK, Dh).transpose(2, 0, 1, 3, 4)
    starts = jnp.arange(nb, dtype=jnp.int32) * Q_BLOCK
    key_pos = jnp.arange(S, dtype=jnp.int32)

    def one_block(args):
        qb, start = args
        z = jnp.einsum('bhqd,bhkd->bhqk', qb, k).astype(jnp.float32) * scale
        q_pos = start + jnp.arange(Q_BLOCK, dtype=jnp.int32)
        causal = key_pos[None, :] < q_pos[:, None]
        log_stay = jnp.where(causal, -jax.nn.softplus(z), 0.0)
        stay_after = lax.cumsum(log_stay, axis=3, reverse=True) - log_stay
        log_w = jax.nn.log_sigmoid(z) + stay_after
        w = jnp.where(causal, jnp.exp(log_w), 0.0)
        return jnp.einsum('bhqk,bhkd->bhqd', w.astype(v.dtype), v)

    out = lax.map(one_block, (q_blocks, starts))
    return out.transpose(1, 2, 0, 3, 4).reshape(B, H, S, Dh)

def conformer_conv(u, g_glu, w_dw, b_dw, ln_g, ln_b, w_pw, b_pw):
    C = u.shape[-1]
    h = u * jax.nn.sigmoid(g_glu)
    h = lax.conv_general_dilated(
        h, w_dw[:, None, :], window_strides=(1,),
        padding=[(CONV_KERNEL - 1, 0)],
        dimension_numbers=('NWC', 'WIO', 'NWC'),
        feature_group_count=C) + b_dw
    h = jax.nn.silu(layer_norm(h, ln_g, ln_b))
    return h @ w_pw + b_pw

def hybrid_layer(x, c, norm_g, w_ada, b_ada, w_in, q_norm_g, k_norm_g,
                 w_dw, b_dw, ln_g, ln_b, w_pw, b_pw, w_out):
    B, S, _ = x.shape
    mod = jax.nn.silu(c) @ w_ada + b_ada
    shift, scale, gate = jnp.split(mod, 3, axis=-1)
    h = rms_norm(x, norm_g) * (1.0 + scale[:, None, :]) + shift[:, None, :]

    proj = h @ w_in
    splits = [SB_WIDTH, 2 * SB_WIDTH, 3 * SB_WIDTH, 4 * SB_WIDTH,
              4 * SB_WIDTH + CONV_WIDTH, 4 * SB_WIDTH + 2 * CONV_WIDTH]
    q, k, v, g_sb, u, g_glu, g_conv = jnp.split(proj, splits, axis=-1)

    def heads(t):
        return t.reshape(B, S, SB_HEADS, HEAD_DIM).transpose(0, 2, 1, 3)

    qh = rms_norm(heads(q), q_norm_g)
    kh = rms_norm(heads(k), k_norm_g)
    o = stick_breaking_attention(qh, kh, heads(v))
    o = o.transpose(0, 2, 1, 3).reshape(B, S, SB_WIDTH)
    y_sb = o * jax.nn.silu(g_sb)

    y_conv = conformer_conv(u, g_glu, w_dw, b_dw, ln_g, ln_b, w_pw, b_pw) * jax.nn.silu(g_conv)

    y = jnp.concatenate([y_sb, y_conv], axis=-1) @ w_out
    return x + gate[:, None, :] * y

def setup_inputs(seed: int = 0) -> dict:
    key = jax.random.key(seed)
    ks = jax.random.split(key, 16)
    f32 = jnp.float32
    D = D_MODEL
    x = jax.random.normal(ks[0], (BATCH, SEQ, D), f32)
    c = jax.random.normal(ks[1], (BATCH, D), f32)
    norm_g = 1.0 + 0.02 * jax.random.normal(ks[2], (DEPTH, D), f32)
    w_ada = 0.5 * D ** -0.5 * jax.random.normal(ks[3], (DEPTH, D, 3 * D), f32)
    b_ada = 0.02 * jax.random.normal(ks[4], (DEPTH, 3 * D), f32)
    w_in = D ** -0.5 * jax.random.normal(ks[5], (DEPTH, D, IN_COLS), f32)
    q_norm_g = 1.0 + 0.02 * jax.random.normal(ks[6], (DEPTH, HEAD_DIM), f32)
    k_norm_g = 1.0 + 0.02 * jax.random.normal(ks[7], (DEPTH, HEAD_DIM), f32)
    w_dw = CONV_KERNEL ** -0.5 * jax.random.normal(ks[8], (DEPTH, CONV_KERNEL, CONV_WIDTH), f32)
    b_dw = 0.02 * jax.random.normal(ks[9], (DEPTH, CONV_WIDTH), f32)
    ln_g = 1.0 + 0.02 * jax.random.normal(ks[10], (DEPTH, CONV_WIDTH), f32)
    ln_b = 0.02 * jax.random.normal(ks[11], (DEPTH, CONV_WIDTH), f32)
    w_pw = CONV_WIDTH ** -0.5 * jax.random.normal(ks[12], (DEPTH, CONV_WIDTH, CONV_WIDTH), f32)
    b_pw = 0.02 * jax.random.normal(ks[13], (DEPTH, CONV_WIDTH), f32)
    w_out = MIX_WIDTH ** -0.5 * jax.random.normal(ks[14], (DEPTH, MIX_WIDTH, D), f32)
    return {"x": x, "c": c, "norm_g": norm_g, "w_ada": w_ada, "b_ada": b_ada,
            "w_in": w_in, "q_norm_g": q_norm_g, "k_norm_g": k_norm_g,
            "w_dw": w_dw, "b_dw": b_dw, "ln_g": ln_g, "ln_b": ln_b,
            "w_pw": w_pw, "b_pw": b_pw, "w_out": w_out}

def reference(x, c, norm_g, w_ada, b_ada, w_in, q_norm_g, k_norm_g,
              w_dw, b_dw, ln_g, ln_b, w_pw, b_pw, w_out):
    for layer in range(DEPTH):
        x = hybrid_layer(x, c, norm_g[layer], w_ada[layer], b_ada[layer], w_in[layer],
                         q_norm_g[layer], k_norm_g[layer], w_dw[layer], b_dw[layer],
                         ln_g[layer], ln_b[layer], w_pw[layer], b_pw[layer], w_out[layer])
    return x


_drawn_inputs = setup_inputs


def setup_inputs(seed=0):
    import zlib

    import numpy as np

    out = dict(_drawn_inputs(seed))
    spreads = {}
    factors = {'norm_g': 8.0,
     'b_ada': 5.255,
     'q_norm_g': 8.0,
     'k_norm_g': 8.0,
     'b_dw': 24.615,
     'ln_g': 41.517,
     'ln_b': 41.516,
     'b_pw': 28.405}
    for name, (base, spread) in spreads.items():
        noise = np.random.default_rng([zlib.crc32(name.encode()), seed]).standard_normal(out[name].shape)
        drawn = base * np.exp(spread * noise) if base else spread * noise
        out[name] = __import__('jax').numpy.asarray(drawn.astype(out[name].dtype))
    for name, factor in factors.items():
        out[name] = (out[name] * factor).astype(out[name].dtype)
    return out
```

```python
import numpy as np
from contextlib import ExitStack

import concourse.bass as bass
from concourse import mybir

F32 = mybir.dt.float32
BF16 = mybir.dt.bfloat16
F32R = mybir.dt.float32r
ACT = mybir.ActivationFunctionType
ALU = mybir.AluOpType

P = 128
D = 4096
T = 256
TT = T // P
HD = 128
SBW = D // 2
CW = D - SBW
TAPS = 31
EPS = 1e-6
NEVER = -2.0 ** 100
ONE = 1
KT = D // P
GC = 1024
NCH = GC // 512
BK = 8
NB = KT // BK
AG = 3 * CW // GC
PAIRS = SBW // (2 * HD)
PG = CW // GC
PKT = CW // P
OG = D // GC
CT = CW // P
SLOTS = 4
HI = 4
LO = 2

BODY = ("w", "a", "w", "a", "w", "a", "w", "a", "e",
        "w", "a", "w", "a", "w", "a", "w", "a", "e",
        "w", "a", "w", "a", "w", "a", "w", "a", "a", "a", "a", "a", "e")
LAST_BODY = ("w", "w", "w", "w", "e") * 3
GROUPS_PER_BODY = 3
BODIES = AG // GROUPS_PER_BODY

ITEM_ADA0 = 4
ITEM_A = ITEM_ADA0 + KT
BODY_ITEMS = BODY.count("w") + BODY.count("a")
LAST_ITEMS = LAST_BODY.count("w")
ITEM_B = ITEM_A + (NB - 1) * BODIES * BODY_ITEMS + BODIES * LAST_ITEMS
ITEM_P = ITEM_B + PAIRS * KT // 2
ITEM_O = ITEM_P + PG * PKT // 2
SUM_A = 4 + KT
SUM_O = 4 + NB * KT
TILE_B = AG * KT
TILE_P = TILE_B + PAIRS * KT
TILE_O = TILE_P + PG * PKT
GROUP_B = AG * NB
GROUP_P = GROUP_B + PAIRS
GROUP_O = GROUP_P + PG

HEAD_STEP = 9


def hybrid_layer(nc, x, c, norm_g, w_ada, b_ada, w_in, q_norm_g, k_norm_g,
                 w_dw, b_dw, ln_g, ln_b, w_pw, b_pw, w_out, out):
    x_rows = x[0].rearrange("(t p) n -> p t n", p=P)
    out_rows = out[0].rearrange("(t p) (g n) -> g p t n", p=P, n=GC)
    ada_rows = w_ada[0].rearrange("(k p) (s b n) -> k p s b n", p=P, s=3, b=NB)
    gate_rows = w_ada[0][:, 2 * D:3 * D].rearrange("(k p) (g n) -> g p k n", p=P, n=GC)
    conv_rows = w_in[0][:, 4 * SBW:].rearrange("(k p) (g n) -> g p k n", p=P, n=GC)
    pair_rows = w_in[0][:, 0:4 * SBW].rearrange("(k p) (r g n) -> g k p r n", p=P, r=4, n=2 * HD)
    pw_rows = w_pw[0].rearrange("(k p) (g n) -> g p k n", p=P, n=GC)
    wo_rows = w_out[0].rearrange("(k p) (g n) -> g p k n", p=P, n=GC)

    ctx = ExitStack()
    with ctx:
        def sb(name, shape, dt=F32):
            return ctx.enter_context(nc.sbuf_tensor(name, shape, dt))

        def bank(name, shape):
            return ctx.enter_context(nc.psum_tensor(name, shape, F32))

        def sem(name):
            return ctx.enter_context(nc.semaphore(name))

        act_hi = sb("act_hi", [P, KT, T], F32R)
        act_lo = sb("act_lo", [P, KT, T], F32R)
        raw = sb("raw", [P, SLOTS, 2, GC])
        whi = sb("whi", [P, HI, GC], F32R)
        wlo = sb("wlo", [P, LO, GC], F32R)
        cbuf = sb("cbuf", [P, AG, TT, GC])
        wide = sb("wide", [P, 2 * GC])
        ysb = sb("ysb", [P, TT, SBW])
        tmp = sb("tmp", [P, 2, 2, T])
        wexp = sb("wexp", [P, 3 * P])
        ident = sb("ident", [P, P])
        neg_tri = sb("neg_tri", [P, P])
        neg_ones = sb("neg_ones", [P, P])
        ones = sb("ones", [P, P])
        never = sb("never", [P, P], BF16)
        ident_b = sb("ident_b", [P, P], BF16)
        cols = sb("cols", [P, 4, KT])
        cols2 = sb("cols2", [P, 64])
        taps = sb("taps", [P, CT, TAPS])
        silu_c = sb("silu_c", [P, KT])
        xstat = sb("xstat", [P, 12])
        mod_mul = sb("mod_mul", [P, BK])
        mod_add = sb("mod_add", [P, BK])
        hstat = sb("hstat", [P, 3, 8])
        sig = sb("sig", [P, TT, 2 * HD])
        ln_stat = sb("ln_stat", [P, T])
        ubuf, glubuf, gatebuf = cbuf[:, 0:2], cbuf[:, 2:4], cbuf[:, 4:6]

        x_block = ysb[:].rearrange("p b (t n) -> p b t n", t=TT)
        h32 = tmp
        qkT = tmp[:, 0]
        absz = tmp[:, 1].rearrange("p a t -> p (a t)")[:, 0:3 * P]
        pair = wide[:].rearrange("p (t n) -> p t n", t=TT)
        conv_in = glubuf.rearrange("p a t n -> p (a t n)").rearrange("p (c t) -> p c t", t=T)
        conv_out = ubuf.rearrange("p a t n -> p (a t n)").rearrange("p (c t) -> p c t", t=T)
        squares = tmp[:].rearrange("p a b (c n) -> p (a b c) n", n=P)
        gate_sum = wide[:, 0:GC]
        gate_bias = wide[0:1, GC:2 * GC]
        gate_sb = tmp[:].rearrange("p a b t -> p (a b t)")
        x_res = cbuf[:, 0]
        y_out = cbuf[:, 2]
        param_rows = raw[:, SLOTS - 1, 0, 0:P]
        param_rows2 = raw[:, SLOTS - 1, 0, P:2 * P]
        tap_rows = cbuf[:, 2].rearrange("p t n -> p (t n)")

        U = bank("U", [P, 4, 512])
        X = [bank(f"X{i}", [P, 512]) for i in range(4)]

        raw_landed = [sem(f"raw_landed{i}") for i in range(SLOTS)]
        params_landed, taps_landed = sem("params_landed"), sem("taps_landed")
        x_landed = [sem("x_landed0"), sem("x_landed1")]
        xres_landed = sem("xres_landed")
        bpw_landed, gbias_landed, stored = sem("bpw_landed"), sem("gbias_landed"), sem("stored")
        item_summed = sem("item_summed")
        hi_ready, lo_ready = sem("hi_ready"), sem("lo_ready")
        hi_slot_free, lo_slot_free = sem("hi_slot_free"), sem("lo_slot_free")
        bank_free = sem("bank_free")
        consts_ready, pool_step = sem("consts_ready"), sem("pool_step")
        params_ps, params_sb, silu_ready = sem("params_ps"), sem("params_sb"), sem("silu_ready")
        ms_ready, rms_ready, rstd_ready = sem("ms_ready"), sem("rms_ready"), sem("rstd_ready")
        dve_step = sem("dve_step")
        mod_summed, wide_zeroed, mod_ready = sem("mod_summed"), sem("wide_zeroed"), sem("mod_ready")
        x_scaled, xT_ps, h_ready = sem("x_scaled"), sem("xT_ps"), sem("h_ready")
        act_hi_ready, act_lo_ready = sem("act_hi_ready"), sem("act_lo_ready")
        gates_ready, glu_ready, gluT_ps, gluT_sb = sem("gates_ready"), sem("glu_ready"), sem("gluT_ps"), sem("gluT_sb")
        conv_step = sem("conv_step")
        sq_ready, hstat_act, hstat_dve, hstat_ready = sem("sq_ready"), sem("hstat_act"), sem("hstat_dve"), sem("hstat_ready")
        eg_ready, sig_step, qk_scaled = sem("eg_ready"), sem("sig_step"), sem("qk_scaled")
        qkT_ps, qkT_sb, z_ps, abs_ready = sem("qkT_ps"), sem("qkT_sb"), sem("z_ps"), sem("abs_ready")
        exp_ready, log_ready, soft_step, soft_ready = sem("exp_ready"), sem("log_ready"), sem("soft_step"), sem("soft_ready")
        logw_ps, w_ready, o_ps, y_done = sem("logw_ps"), sem("w_ready"), sem("o_ps"), sem("y_done")
        mean_ps, xc_ready, sqc_ready, var_ps = sem("mean_ps"), sem("xc_ready"), sem("sqc_ready"), sem("var_ps")
        var_ready, deviation_ready = sem("var_ready"), sem("deviation_ready")
        norm_ready, swish_ready = sem("norm_ready"), sem("swish_ready")
        conv_hi, conv_lo = sem("conv_hi"), sem("conv_lo")
        ysbT_ps, ysb_hi, ysb_lo = sem("ysbT_ps"), sem("ysb_hi"), sem("ysb_lo")
        ycT_ps, yc_hi, yc_lo = sem("ycT_ps"), sem("yc_hi"), sem("yc_lo")
        gate_step, gate_ps, gate_ready = sem("gate_step"), sem("gate_ps"), sem("gate_ready")
        out_ready, y_out_free = sem("out_ready"), sem("y_out_free")

        block = ctx.enter_context(nc.Block())

        @block.sync
        def _(sp):
            def load(slot, dst, src, summed=None, split=None):
                if summed is not None:
                    sp.wait_ge(item_summed, summed)
                if split is not None:
                    if not isinstance(split, int):
                        split = sp.snap(split)
                        sp.wait_ge(params_ps, 1)
                    sp.wait_ge(lo_ready, split)
                sp.dma_start(dst, src).then_inc(raw_landed[slot], 16)

            def load_x(b):
                if b >= 2:
                    sp.wait_ge(xT_ps, BK // 2 * (b - 1))
                sp.dma_start(x_block[:, b % 2], x_rows[:, :, b * BK * P:(b + 1) * BK * P]).then_inc(x_landed[b % 2], 16)

            for n in range(SLOTS):
                if n == SLOTS - 1:
                    sp.wait_ge(params_ps, 1)
                sp.dma_start(raw[:, n].rearrange("p a n -> p (a n)"),
                             x_rows[:, n // 2, n % 2 * 2 * GC:(n % 2 + 1) * 2 * GC]).then_inc(raw_landed[n], 16)
            for k in range(KT):
                n = ITEM_ADA0 + k
                load(n % SLOTS, raw[:, n % SLOTS], ada_rows[k, :, 0:2, 0, :], summed=n - SLOTS + 1)
                if k == 8:
                    load_x(0)
                if k == 16:
                    load_x(1)
            kinds = [kind for kind in BODY if kind != "e"]
            for b in range(NB - 1):
                if b >= 1:
                    load_x(b + 1)
                with sp.Fori(0, BODIES) as it:
                    w_items = a_items = 0
                    for n, kind in enumerate(kinds):
                        before = kinds[:max(n - SLOTS + 1, 0)]
                        if n < SLOTS or kinds[n - SLOTS] == "a":
                            wait = dict(summed=SUM_A + KT * b + it * (KT // BODIES) + before.count("a")
                                        - max(SLOTS - 1 - n, 0))
                        else:
                            wait = dict(split=BK * AG * b + it * (BK * GROUPS_PER_BODY) + 2 * before.count("w"))
                        slot = n % SLOTS
                        if kind == "w":
                            g, kp = w_items // (BK // 2), w_items % (BK // 2)
                            k0 = b * BK + 2 * kp
                            load(slot, raw[:, slot], conv_rows[it * GROUPS_PER_BODY + g, :, k0:k0 + 2, :], **wait)
                            w_items += 1
                        else:
                            load(slot, raw[:, slot], ada_rows[it * (KT // BODIES) + a_items, :, 0:2, b + 1, :], **wait)
                            a_items += 1
            for n in range(AG * BK // 2):
                g, k0 = n // (BK // 2), (NB - 1) * BK + 2 * (n % (BK // 2))
                wait = dict(summed=SUM_O - (SLOTS - 1 - n)) if n < SLOTS else \
                    dict(split=BK * AG * (NB - 1) + 2 * (n - SLOTS + 1))
                load(n % SLOTS, raw[:, n % SLOTS], conv_rows[g, :, k0:k0 + 2, :], **wait)

            def load_pair(g):
                for kp in range(KT // 2):
                    split = TILE_B + g * KT + 2 * (kp - SLOTS + 1)
                    sp.wait_ge(lo_ready, split)
                    for kk in range(2):
                        sp.dma_start(raw[:, kp % SLOTS, kk].rearrange("p (r n) -> p r n", r=4),
                                     pair_rows[g, 2 * kp + kk]).then_inc(raw_landed[kp % SLOTS], 16)

            load_pair(0)
            with sp.Fori(1, PAIRS) as g:
                load_pair(g)
            for g in range(PG):
                for kp in range(PKT // 2):
                    n = g * (PKT // 2) + kp
                    load(n % SLOTS, raw[:, n % SLOTS], pw_rows[g, :, 2 * kp:2 * kp + 2, :],
                         split=TILE_P + 2 * (n - SLOTS + 1))
            with sp.Fori(0, OG) as g:
                for n in range(KT):
                    if n % 2 == 0 and n >= SLOTS:
                        wait = dict(summed=SUM_O + g * (KT // 2) + n // 2 - 1)
                    else:
                        wait = dict(split=TILE_O + g * KT + 2 * (n // 2 - 1))
                    rows = gate_rows if n % 2 == 0 else wo_rows
                    k0 = n // 2 * 2
                    load(n % SLOTS, raw[:, n % SLOTS], rows[g, :, k0:k0 + 2, :], **wait)

        def landed(item):
            return 16 * (item // SLOTS + 1)

        def landed_b(g, kp):
            return 16 * (ITEM_B // SLOTS) + (KT // 2 // SLOTS) * 32 * g + 32 * (kp // SLOTS + 1)

        EXTRA = 16 * (PAIRS * KT // 2 // SLOTS)

        @block.tensor
        def _(pe):
            pe.sem_inc(hi_slot_free, HI)
            pe.sem_inc(lo_slot_free, LO)
            for s in (z_ps, logw_ps, o_ps, gate_ps):
                pe.sem_inc(s, ONE)

            def k_tile(tile, count, slot, group=None, first=False, last=False, seeded=False):
                hi, lo = whi[:, slot % HI], wlo[:, slot % LO]
                pe.wait_ge(hi_ready, count + 1)
                for t in range(TT):
                    for part in (act_hi, act_lo):
                        for ch in range(NCH):
                            if first and not seeded and part is act_hi:
                                pe.wait_ge(bank_free, 4 * group + t * NCH + ch + 1)
                            nc.tensor.matmul(U[:, t * NCH + ch], part[:, tile, t * P:(t + 1) * P],
                                             hi[:, ch * 512:(ch + 1) * 512],
                                             start=first and not seeded and part is act_hi, stop=False)
                pe.wait_ge(lo_ready, count + 1)
                for t in range(TT):
                    for ch in range(NCH):
                        m = nc.tensor.matmul(U[:, t * NCH + ch], act_hi[:, tile, t * P:(t + 1) * P],
                                             lo[:, ch * 512:(ch + 1) * 512], start=False, stop=last)
                        if t == 0 and ch == 0:
                            m.then_inc(hi_slot_free, 1)
                m.then_inc(lo_slot_free, 1)

            pe.wait_ge(consts_ready, 1)
            pe.wait_ge(params_landed, 16 * 9)
            nc.tensor.transpose(X[0][:, 0:P], param_rows, ident[:])
            nc.tensor.transpose(X[0][:, P:2 * P], param_rows2, ident[:]).then_inc(params_ps, 1)
            pe.wait_ge(taps_landed, 16)
            for ct in range(CT):
                m = nc.tensor.transpose(X[1][:, ct * TAPS:(ct + 1) * TAPS], tap_rows[0:TAPS, ct * P:(ct + 1) * P],
                                        ident[0:TAPS, 0:TAPS])
            m.then_inc(params_ps, 1)
            pe.wait_ge(params_sb, 2)

            def modulate(b):
                pe.wait_ge(item_summed, 4 + KT * (b + 1))
                for s in range(2):
                    for j in range(BK):
                        m = nc.tensor.matmul(X[3][:, s * BK + j:s * BK + j + 1],
                                             wide[:, s * GC + j * P:s * GC + (j + 1) * P], ones[:, 0:1],
                                             start=True, stop=True)
                m.then_inc(mod_summed, 1)
                pe.wait_ge(x_scaled, 2 * (b + 1))
                for q in range(BK // 2):
                    n = b * (BK // 2) + q
                    if n >= 2:
                        pe.wait_ge(h_ready, n - 1)
                    for kk in range(2):
                        for t in range(TT):
                            k = 2 * q + kk
                            m = nc.tensor.transpose(X[q % 2][:, kk * T + t * P:kk * T + (t + 1) * P],
                                                    x_block[:, b % 2, t, k * P:(k + 1) * P], ident[:])
                    m.then_inc(xT_ps, 1)
                pe.wait_ge(act_lo_ready, (b + 1) * (BK // 2))
                pe.wait_ge(act_hi_ready, (b + 1) * (BK // 2))

            for b in range(NB):
                modulate(b)
                with pe.Fori(0, BODIES) as it:
                    for g in range(GROUPS_PER_BODY):
                        for k in range(BK):
                            count = AG * BK * b + it * (GROUPS_PER_BODY * BK) + g * BK + k
                            k_tile(b * BK + k, count, k, AG * b + it * GROUPS_PER_BODY + g,
                                   first=k == 0, last=k == BK - 1)

            def glu_transpose(r):
                if r == 0:
                    pe.wait_ge(glu_ready, 4)
                if r >= 2:
                    pe.wait_ge(gluT_sb, r - 1)
                for kk in range(2):
                    ct = 2 * r + kk
                    for t in range(TT):
                        m = nc.tensor.transpose(X[r % 2][:, kk * T + t * P:kk * T + (t + 1) * P],
                                                ubuf[:, ct // 8, t, ct % 8 * P:(ct % 8 + 1) * P], ident[:])
                m.then_inc(gluT_ps, 1)

            def attend(step, h, local):
                if step == "transpose":
                    pe.wait_ge(qk_scaled, h + 1)
                    pe.wait_ge(qkT_sb, ONE + h)
                    for s in range(2):
                        for t in range(TT):
                            m = nc.tensor.transpose(X[3][:, s * T + t * P:s * T + (t + 1) * P],
                                                    pair[:, t, (2 * s + local) * HD:(2 * s + local + 1) * HD], ident[:])
                    m.then_inc(qkT_ps, 1)
                if step == "z":
                    pe.wait_ge(qkT_sb, ONE + h + 1)
                    pe.wait_ge(w_ready, ONE + h)
                    nc.tensor.matmul(X[1][:, 0:T], qkT[:, 1, 0:P], qkT[:, 0, :], start=True, stop=False,
                                     skip_group_check=True)
                    nc.tensor.matmul(X[1][:, T:T + P], qkT[:, 1, P:T], qkT[:, 0, P:T], start=False, stop=False,
                                     skip_group_check=True)
                    for diagonal in (0, T):
                        m = nc.tensor.matmul(X[1][:, diagonal:diagonal + P], ident_b[:], never[:], start=False,
                                             stop=False, skip_group_check=True)
                    m.then_inc(z_ps, 1)
                if step == "sum":
                    pe.wait_ge(soft_ready, h + 1)
                    nc.tensor.matmul(X[1][:, 0:T], neg_tri[:], absz[:, 0:T], start=False, stop=False,
                                     skip_group_check=True)
                    nc.tensor.matmul(X[1][:, P:T], neg_ones[:], absz[:, T:T + P], start=False, stop=False,
                                     skip_group_check=True)
                    nc.tensor.matmul(X[1][:, T:T + P], neg_tri[:], absz[:, T:T + P], start=False, stop=True,
                                     skip_group_check=True).then_inc(logw_ps, 1)
                if step == "o":
                    v = (4 + local) * HD
                    pe.wait_ge(w_ready, ONE + h + 1)
                    pe.wait_ge(y_done, ONE + h)
                    nc.tensor.matmul(X[2][:, 0:P], wexp[:, 0:P], pair[:, 0, v:v + HD], start=True, stop=True)
                    nc.tensor.matmul(X[2][:, P:T], wexp[:, P:T], pair[:, 0, v:v + HD], start=False, stop=False,
                                     skip_group_check=True)
                    nc.tensor.matmul(X[2][:, P:T], wexp[:, T:T + P], pair[:, 1, v:v + HD], start=False, stop=True,
                                     skip_group_check=True).then_inc(o_ps, 1)

            PE_STEPS = {8: ("transpose", 0), 10: ("z", 0), 14: ("sum", 0), 16: ("transpose", 1), 17: ("o", 0),
                        19: ("z", 1), 23: ("sum", 1), 26: ("o", 1)}
            for k in range(KT):
                k_tile(k, TILE_B + k, k, GROUP_B, first=k == 0, last=k == KT - 1)
                if 4 <= k < 4 + CT // 2:
                    glu_transpose(k - 4)
            with pe.Fori(1, PAIRS) as g:
                for k in range(KT):
                    k_tile(k, TILE_B + g * KT + k, k, GROUP_B + g, first=k == 0, last=k == KT - 1)
                    if k in PE_STEPS:
                        step, local = PE_STEPS[k]
                        attend(step, (g - 1) * 2 + local, local)

            last = 2 * (PAIRS - 1)
            attend("transpose", last, 0)
            attend("z", last, 0)
            pe.wait_ge(conv_step, CT * TAPS)
            pe.wait_ge(gluT_sb, CT // 2)
            for ct in range(CT):
                m = nc.tensor.matmul(X[0][:, 0:T], neg_ones[:], conv_out[:, ct], start=ct == 0, stop=ct == CT - 1)
            m.then_inc(mean_ps, 1)
            attend("sum", last, 0)
            attend("transpose", last + 1, 1)
            attend("o", last, 0)
            attend("z", last + 1, 1)
            for ct in range(CT):
                if ct % 4 == 0:
                    pe.wait_ge(sqc_ready, ct // 4 + 1)
                    if ct == 0:
                        pe.wait_ge(xc_ready, 1)
                m = nc.tensor.matmul(X[0][:, 0:T], ones[:], conv_in[:, ct], start=ct == 0, stop=ct == CT - 1)
            m.then_inc(var_ps, 1)
            attend("sum", last + 1, 1)
            attend("o", last + 1, 1)

            def y_transpose(r, source, seen, free, ready):
                pe.wait_ge(seen[0], seen[1])
                if r >= 2:
                    pe.wait_ge(free, r - 1)
                for kk in range(2):
                    for t in range(TT):
                        m = nc.tensor.transpose(X[r % 2][:, kk * T + t * P:kk * T + (t + 1) * P],
                                                source(2 * r + kk, t), ident[:])
                m.then_inc(ready, 1)

            pe.wait_ge(bpw_landed, 16)
            pe.wait_ge(var_ready, 1)
            for g in range(PG):
                for t in range(TT):
                    for ch in range(NCH):
                        pe.wait_ge(bank_free, 4 * (GROUP_P + g) + t * NCH + ch + 1)
                        nc.tensor.matmul(U[:, t * NCH + ch], ones[0:1, :],
                                         wide[0:1, g * GC + ch * 512:g * GC + (ch + 1) * 512], start=True, stop=False)
                for k in range(PKT):
                    if g == 0:
                        pe.wait_ge(conv_lo, k // 2 + 1)
                    k_tile(k, TILE_P + g * PKT + k, k, last=k == PKT - 1, first=k == 0, seeded=True)
                    s = g * PKT + k
                    if s >= 4 and s % 2 == 0 and s < 4 + CT:
                        r = (s - 4) // 2
                        y_transpose(r, lambda kt, t: ysb[:, t, kt * P:(kt + 1) * P], (y_done, ONE + 2 * PAIRS), ysb_lo, ysbT_ps)

            pe.wait_ge(ysb_lo, CT // 2)
            for r in range(CT // 2):
                y_transpose(r, lambda kt, t: gatebuf[:, kt // 8, t, kt % 8 * P:(kt % 8 + 1) * P],
                            (bank_free, 4 * (GROUP_P + (r // 4) + 1) + 4), yc_lo, ycT_ps)

            with pe.Fori(0, OG) as g:
                for k in range(KT):
                    if k == KT // 2:
                        pe.wait_ge(yc_lo, CT // 2)
                    k_tile((k + KT // 2) % KT, TILE_O + g * KT + k, k, GROUP_O + g, first=k == 0, last=k == KT - 1)
                    if k == KT - 2:
                        pe.wait_ge(item_summed, SUM_O + (g + 1) * (KT // 2))
                        pe.wait_ge(gbias_landed, 16 * (g + 1))
                        pe.wait_ge(gate_ready, ONE + 2 * g)
                        for ch in range(NCH):
                            nc.tensor.matmul(X[2 + ch][:], ones[:], gate_sum[:, ch * 512:(ch + 1) * 512], start=True, stop=False)
                            m = nc.tensor.matmul(X[2 + ch][:], ones[0:1, :], gate_bias[:, ch * 512:(ch + 1) * 512],
                                                 start=False, stop=True)
                        m.then_inc(gate_ps, 1)

        @block.scalar
        def _(act):
            def copy(dst, src):
                return nc.scalar.activation(dst, src, ACT.Copy)

            def high(count, slot, item_slot, kk, lands):
                act.wait_ge(raw_landed[item_slot], lands)
                act.wait_ge(hi_slot_free, count + 1)
                copy(whi[:, slot % HI], raw[:, item_slot, kk]).then_inc(hi_ready, 1)

            for s in (qkT_sb, w_ready, gate_ready):
                act.sem_inc(s, ONE)

            act.wait_ge(pool_step, 1)
            for n, v in enumerate((c[0], norm_g[0], b_ada[0, 0:D], b_ada[0, D:2 * D])):
                act.dma_start(param_rows[n * KT:(n + 1) * KT, :], v.rearrange("(k p) -> k p", p=P)).then_inc(params_landed, 16)
            for n, v in enumerate((ln_g[0], ln_b[0], b_dw[0])):
                act.dma_start(param_rows2[n * CT:(n + 1) * CT, :], v.rearrange("(k p) -> k p", p=P)).then_inc(params_landed, 16)
            act.dma_start(param_rows2[3 * CT:3 * CT + 1, :], q_norm_g).then_inc(params_landed, 16)
            act.dma_start(param_rows2[3 * CT + 1:3 * CT + 2, :], k_norm_g).then_inc(params_landed, 16)
            act.dma_start(tap_rows[0:TAPS, :], w_dw[0]).then_inc(taps_landed, 16)
            act.wait_ge(params_sb, 1)
            nc.scalar.activation(silu_c[:], cols[:, 0], ACT.Silu).then_inc(silu_ready, 1)
            act.wait_ge(ms_ready, 1)
            nc.scalar.activation(xstat[:, 6:8], xstat[:, 4:6], ACT.Sqrt).then_inc(rms_ready, 1)

            def modulate(b):
                act.wait_ge(x_landed[b % 2], 16 * (b // 2 + 1))
                act.wait_ge(rstd_ready, 1)
                for t in range(TT):
                    nc.scalar.activation(x_block[:, b % 2, t], x_block[:, b % 2, t], ACT.Copy,
                                         scale=xstat[:, 8 + t:9 + t]).then_inc(x_scaled, 1)
                for q in range(BK // 2):
                    act.wait_ge(h_ready, b * (BK // 2) + q + 1)
                    copy(act_hi[:, b * BK + 2 * q:b * BK + 2 * q + 2], h32[:, q % 2]).then_inc(act_hi_ready, 1)

            for b in range(NB):
                modulate(b)
                body = BODY if b < NB - 1 else LAST_BODY
                kinds = [kind for kind in body if kind != "e"]
                with act.Fori(0, BODIES) as it:
                    w_tiles = 0
                    for n, kind in enumerate(kinds):
                        if kind == "w":
                            for kk in range(2):
                                high(AG * BK * b + it * (GROUPS_PER_BODY * BK) + w_tiles, w_tiles, n % SLOTS, kk,
                                     landed(ITEM_A + b * BODIES * BODY_ITEMS + n) + it * (len(kinds) // SLOTS * 16))
                                w_tiles += 1

            def pair_tile(g, k):
                high(TILE_B + g * KT + k, k, k // 2 % SLOTS, k % 2, landed_b(g, k // 2))

            def prepare_pair(step, g):
                if step == "squares":
                    act.wait_ge(bank_free, 4 * (GROUP_B + g + 1) + 4)
                    act.wait_ge(hstat_ready, ONE + g)
                    act.wait_ge(o_ps, ONE + 2 * g)
                    for t in range(TT):
                        for j in range(4):
                            i = nc.scalar.activation(squares[:, t * 4 + j], pair[:, t, j * HD:(j + 1) * HD], ACT.Square,
                                                     accum_out=hstat[:, 0, t * 4 + j:t * 4 + j + 1])
                            i.then_inc(sq_ready, 1)
                if step == "roots":
                    act.wait_ge(hstat_dve, 4 * g + 1)
                    nc.scalar.activation(hstat[:, 1], hstat[:, 0], ACT.Ln).then_inc(hstat_act, 1)
                    act.wait_ge(hstat_act, 2 * g + 1)
                    nc.scalar.activation(hstat[:, 1], hstat[:, 1], ACT.Exp, scale=-0.5).then_inc(hstat_act, 1)
                if step == "gate":
                    act.wait_ge(y_done, ONE + 2 * g)
                    nc.scalar.activation(sig[:], pair[:, :, 6 * HD:8 * HD], ACT.Exp, scale=-1.0).then_inc(eg_ready, 1)

            def attend(step, h, local):
                if step == "scale":
                    for t in range(TT):
                        for s in range(2):
                            j = 2 * s + local
                            seg = pair[:, t, j * HD:(j + 1) * HD]
                            i = nc.scalar.activation(seg, seg, ACT.Copy, scale=hstat[:, 2, t * 4 + j:t * 4 + j + 1])
                    i.then_inc(qk_scaled, 1)
                if step == "gains":
                    act.wait_ge(qkT_ps, h + 1)
                    act.wait_ge(z_ps, ONE + h)
                    nc.scalar.activation(qkT[:, 0], X[3][:, 0:T], ACT.Copy, scale=cols2[:, 3 * CT:3 * CT + 1])
                    nc.scalar.activation(qkT[:, 1], X[3][:, T:2 * T], ACT.Copy,
                                         scale=cols2[:, 3 * CT + 1:3 * CT + 2]).then_inc(qkT_sb, 1)
                if step == "soft":
                    act.wait_ge(z_ps, ONE + h + 1)
                    act.wait_ge(logw_ps, ONE + h)
                    nc.scalar.activation(absz, X[1][:, 0:3 * P], ACT.Abs).then_inc(abs_ready, 1)
                    act.wait_ge(abs_ready, h + 1)
                    nc.scalar.activation(absz[:], absz[:], ACT.Exp, scale=-1.0).then_inc(exp_ready, 1)
                    act.wait_ge(exp_ready, h + 1)
                    nc.scalar.activation(absz[:], absz[:], ACT.Ln, bias=1.0).then_inc(log_ready, 1)
                if step == "w":
                    act.wait_ge(logw_ps, ONE + h + 1)
                    act.wait_ge(o_ps, ONE + h)
                    nc.scalar.activation(wexp[:], X[1][:, 0:3 * P], ACT.Exp).then_inc(w_ready, 1)

            ACT_PREP = {4: "squares", 5: "roots", 6: "gate"}
            ACT_STEPS = {8: ("scale", 0), 12: ("gains", 0), 10: ("scale", 1), 15: ("soft", 0), 18: ("w", 0),
                         20: ("gains", 1), 24: ("soft", 1), 27: ("w", 1)}

            def glu_gates(n):
                if n < 4:
                    piece = glubuf[:, n // 2, n % 2]
                    nc.scalar.activation(piece, piece, ACT.Sigmoid).then_inc(gates_ready, 1)
                else:
                    piece = gatebuf[:, n // 2 - 2, n % 2]
                    nc.scalar.activation(piece, piece, ACT.Silu).then_inc(gates_ready, 1)

            for k in range(KT):
                pair_tile(0, k)
                if k == 0:
                    act.wait_ge(bank_free, 4 * GROUP_B + 4)
                if k < 8:
                    glu_gates(k)
                if 8 <= k < 8 + CT // 2:
                    r = k - 8
                    act.wait_ge(gluT_ps, r + 1)
                    copy(conv_in[:, 2 * r:2 * r + 2].rearrange("p c t -> p (c t)"), X[r % 2][:]).then_inc(gluT_sb, 1)
            with act.Fori(1, PAIRS) as g:
                for k in range(KT):
                    pair_tile(g, k)
                    if k in ACT_PREP:
                        prepare_pair(ACT_PREP[k], g - 1)
                    if k in ACT_STEPS:
                        step, local = ACT_STEPS[k]
                        if step == "scale":
                            act.wait_ge(hstat_ready, ONE + g)
                        attend(step, (g - 1) * 2 + local, local)

            last = 2 * (PAIRS - 1)
            for step in ("squares", "roots", "gate"):
                prepare_pair(step, PAIRS - 1)
            act.wait_ge(hstat_ready, ONE + PAIRS)
            attend("scale", last, 0)
            attend("scale", last + 1, 1)
            attend("gains", last, 0)
            attend("soft", last, 0)
            attend("w", last, 0)
            attend("gains", last + 1, 1)
            for n in range(4):
                act.wait_ge(xc_ready, n + 2)
                nc.scalar.activation(conv_in[:, 4 * n:4 * n + 4], conv_out[:, 4 * n:4 * n + 4], ACT.Square).then_inc(sqc_ready, 1)
            attend("soft", last + 1, 1)
            attend("w", last + 1, 1)
            act.wait_ge(var_ready, 1)
            nc.scalar.activation(ln_stat[:], ln_stat[:], ACT.Sqrt).then_inc(deviation_ready, 1)

            def swish(ct):
                if ct % 4 == 0:
                    act.wait_ge(norm_ready, ct // 4 + 1)
                nc.scalar.activation(conv_out[:, ct], conv_out[:, ct], ACT.Silu, scale=cols2[:, ct:ct + 1],
                                     bias=cols2[:, CT + ct:CT + ct + 1]).then_inc(swish_ready, 1)
                if ct % 2 == 1:
                    act.wait_ge(swish_ready, ct + 1)
                    copy(act_hi[:, ct - 1:ct + 1], conv_out[:, ct - 1:ct + 1]).then_inc(conv_hi, 1)

            for ct in range(CT):
                swish(ct)

            def y_high(r, ps, ready, tile, free=None):
                act.wait_ge(ps, r + 1)
                copy(act_hi[:, tile:tile + 2].rearrange("p c t -> p (c t)"), X[r % 2][:]).then_inc(ready, 1)

            for s in range(PG * PKT):
                n = s // 2
                high(TILE_P + s, s, n % SLOTS, s % 2, landed(ITEM_P + n) + EXTRA)
                if s >= 8 and s % 2 == 0 and s < 8 + CT:
                    r = (s - 8) // 2
                    y_high(r, ysbT_ps, ysb_hi, KT // 2 + 2 * r)
            act.wait_ge(bank_free, 4 * (GROUP_P + 2) + 4)
            for r in range(CT // 2):
                y_high(r, ycT_ps, yc_hi, 2 * r)
            with act.Fori(0, OG) as g:
                for n in range(1, KT, 2):
                    for kk in range(2):
                        k = n - 1 + kk
                        high(TILE_O + g * KT + k, k, n % SLOTS, kk,
                             landed(ITEM_O + n) + EXTRA + g * (KT // SLOTS * 16))
                act.wait_ge(gate_ps, ONE + g + 1)
                act.wait_ge(bank_free, 4 * (GROUP_O + g) + 4)
                for ch in range(NCH):
                    copy(gate_sb[:, ch * 512:(ch + 1) * 512], X[2 + ch][:]).then_inc(gate_ready, 1)

        @block.gpsimd
        def _(pool):
            nc.gpsimd.memset(param_rows2, 0.0).then_inc(pool_step, 1)
            for n, (dst, value) in enumerate(((ident, 0.0), (neg_tri, -1.0), (neg_ones, -1.0), (ones, 1.0), (never, 0.0), (ident_b, 0.0))):
                nc.gpsimd.memset(dst[:], value).then_inc(pool_step, 1)
            pool.wait_ge(pool_step, 7)
            nc.gpsimd.affine_select(out=ident[:], in_=ident[:], compare_op=ALU.not_equal, fill=1.0, base=0,
                                    pattern=[[-1, P]], channel_multiplier=1).then_inc(pool_step, 1)
            nc.gpsimd.affine_select(out=neg_tri[:], in_=neg_tri[:], compare_op=ALU.is_ge, fill=0.0, base=0,
                                    pattern=[[-1, P]], channel_multiplier=1).then_inc(pool_step, 1)
            nc.gpsimd.affine_select(out=never[:], in_=never[:], compare_op=ALU.is_gt, fill=NEVER, base=0,
                                    pattern=[[1, P]], channel_multiplier=-1).then_inc(pool_step, 1)
            nc.gpsimd.affine_select(out=ident_b[:], in_=ident_b[:], compare_op=ALU.not_equal, fill=1.0, base=0,
                                    pattern=[[-1, P]], channel_multiplier=1).then_inc(pool_step, 1)
            pool.wait_ge(pool_step, 11)
            nc.gpsimd.memset(wide[:], 0.0).then_inc(wide_zeroed, 1)
            pool.wait_ge(wide_zeroed, 1)
            pool.sem_inc(consts_ready, 1)
            for b in range(NB - 1):
                pool.wait_ge(mod_summed, b + 1)
                nc.gpsimd.memset(wide[:], 0.0).then_inc(wide_zeroed, 1)

            pool.wait_ge(o_ps, ONE + 2 * PAIRS)
            pool.wait_ge(eg_ready, PAIRS)
            pool.wait_ge(y_done, ONE + 2 * PAIRS)
            pool.dma_start(wide[0:1, 0:CW], b_pw).then_inc(bpw_landed, 16)
            pool.wait_ge(bank_free, 4 * (GROUP_P + PG) + 4)
            pool.wait_ge(conv_lo, CT // 2)
            for g in range(OG):
                pool.wait_ge(out_ready, g)
                pool.dma_start(x_res, x[0].rearrange("(t p) (g n) -> g p t n", p=P, n=GC)[g]).then_inc(xres_landed, 16)
                pool.wait_ge(gate_ps, ONE + g)
                pool.dma_start(gate_bias, b_ada[:, 2 * D:3 * D].rearrange("o (g n) -> g o n", n=GC)[g]).then_inc(gbias_landed, 16)
                pool.wait_ge(out_ready, g + 1)
                pool.dma_start(out_rows[g], y_out).then_inc(stored, 16)
                pool.wait_ge(stored, 16 * (g + 1))
                pool.sem_inc(y_out_free, 1)

        @block.vector
        def _(dve):
            dve.sem_inc(bank_free, 4)
            for s in (y_done, hstat_ready):
                dve.sem_inc(s, ONE)
            dve.sem_inc(y_out_free, ONE)
            steps = [0]

            def then(instruction):
                steps[0] += 1
                instruction.then_inc(dve_step, 1)
                dve.wait_ge(dve_step, steps[0])

            def low(count, slot, item_slot, kk):
                dve.wait_ge(hi_ready, count + 1)
                dve.wait_ge(lo_slot_free, count + 1)
                nc.vector.tensor_tensor(wlo[:, slot % LO], raw[:, item_slot, kk],
                                        whi[:, slot % HI].bitcast(F32), ALU.subtract).then_inc(lo_ready, 1)

            dve.wait_ge(params_ps, 1)
            nc.vector.tensor_copy(cols[:].rearrange("p a k -> p (a k)"), X[0][:, 0:P])
            then(nc.vector.tensor_copy(cols2[:], X[0][:, P:P + 64]))
            nc.vector.tensor_scalar(cols2[:, 3 * CT:3 * CT + 1], cols2[:, 3 * CT:3 * CT + 1], HD ** -0.5, None,
                                    ALU.mult).then_inc(params_sb, 1)
            dve.wait_ge(params_ps, 2)
            nc.vector.tensor_copy(taps[:].rearrange("p c k -> p (c k)"), X[1][:, 0:CT * TAPS]).then_inc(params_sb, 1)
            for n in range(4):
                dve.wait_ge(raw_landed[n], 16)
                piece = raw[:, n].rearrange("p a n -> p (a n)")
                nc.vector.tensor_tensor_reduce(out=piece, in0=piece, in1=piece, scale=1.0, scalar=0.0, op0=ALU.mult,
                                               op1=ALU.add, accum_out=xstat[:, n:n + 1]).then_inc(item_summed, 1)
            dve.wait_ge(item_summed, 4)
            halves = xstat[:, 0:4].rearrange("p (t h) -> p t h", h=2)
            then(nc.vector.tensor_tensor(xstat[:, 4:6], halves[:, :, 0], halves[:, :, 1], ALU.add))
            nc.vector.tensor_scalar(xstat[:, 4:6], xstat[:, 4:6], 1.0 / D, EPS, ALU.mult, ALU.add).then_inc(ms_ready, 1)
            dve.wait_ge(rms_ready, 1)
            nc.vector.reciprocal(xstat[:, 8:10], xstat[:, 6:8]).then_inc(rstd_ready, 1)
            dve.wait_ge(silu_ready, 1)
            dve.wait_ge(wide_zeroed, 1)

            def ada(k, item_slot, lands, summed):
                dve.wait_ge(raw_landed[item_slot], lands)
                dve.wait_ge(item_summed, summed)
                nc.vector.scalar_tensor_tensor(out=wide[:], in0=raw[:, item_slot].rearrange("p a n -> p (a n)"),
                                               scalar=k, in1=wide[:], op0=ALU.mult, op1=ALU.add).then_inc(item_summed, 1)

            for k in range(KT):
                n = ITEM_ADA0 + k
                ada(silu_c[:, k:k + 1], n % SLOTS, landed(n), n)

            def modulate(b):
                dve.wait_ge(mod_summed, b + 1)
                ks = slice(b * BK, (b + 1) * BK)
                nc.vector.tensor_tensor(mod_add[:], X[3][:, 0:BK], cols[:, 2, ks], ALU.add)
                then(nc.vector.tensor_tensor(mod_mul[:], X[3][:, BK:2 * BK], cols[:, 3, ks], ALU.add))
                then(nc.vector.scalar_tensor_tensor(out=mod_mul[:], in0=mod_mul[:], scalar=1.0, in1=cols[:, 1, ks],
                                                    op0=ALU.add, op1=ALU.mult))

                def affine(q):
                    n = b * (BK // 2) + q
                    dve.wait_ge(xT_ps, n + 1)
                    if n >= 2:
                        dve.wait_ge(act_hi_ready, n - 1)
                        dve.wait_ge(act_lo_ready, n - 1)
                    for kk in range(2):
                        k = 2 * q + kk
                        i = nc.vector.tensor_scalar(h32[:, q % 2, kk], X[q % 2][:, kk * T:(kk + 1) * T],
                                                    mod_mul[:, k:k + 1], mod_add[:, k:k + 1], ALU.mult, ALU.add)
                    i.then_inc(h_ready, 1)

                def lo(q):
                    dve.wait_ge(act_hi_ready, b * (BK // 2) + q + 1)
                    dve.wait_ge(h_ready, b * (BK // 2) + q + 1)
                    ks = slice(b * BK + 2 * q, b * BK + 2 * q + 2)
                    nc.vector.tensor_tensor(act_lo[:, ks], h32[:, q % 2], act_hi[:, ks].bitcast(F32),
                                            ALU.subtract).then_inc(act_lo_ready, 1)

                affine(0)
                for q in range(1, BK // 2):
                    affine(q)
                    lo(q - 1)
                lo(BK // 2 - 1)

            for b in range(NB):
                modulate(b)
                if b < NB - 1:
                    dve.wait_ge(wide_zeroed, b + 2)
                body = BODY if b < NB - 1 else LAST_BODY
                items = len([kind for kind in body if kind != "e"])
                with dve.Fori(0, BODIES) as it:
                    n = w_tiles = a_items = g = 0
                    for kind in body:
                        if kind == "w":
                            for kk in range(2):
                                low(AG * BK * b + it * (GROUPS_PER_BODY * BK) + w_tiles, w_tiles, n % SLOTS, kk)
                                w_tiles += 1
                            n += 1
                        elif kind == "a":
                            k = it * (KT // BODIES) + a_items
                            ada(silu_c[:, bass.ds(k, 1)], n % SLOTS,
                                landed(ITEM_A + b * BODIES * BODY_ITEMS + n) + it * (items // SLOTS * 16),
                                SUM_A + KT * b + k)
                            a_items += 1
                            n += 1
                        else:
                            dve.wait_ge(lo_slot_free, AG * BK * b + it * (GROUPS_PER_BODY * BK) + (g + 1) * BK + LO)
                            for t in range(TT):
                                for ch in range(NCH):
                                    dst = cbuf[:, it * GROUPS_PER_BODY + g, t, ch * 512:(ch + 1) * 512]
                                    if b == 0:
                                        nc.vector.tensor_copy(dst, U[:, t * NCH + ch]).then_inc(bank_free, 1)
                                    else:
                                        nc.vector.tensor_tensor(dst, dst, U[:, t * NCH + ch], ALU.add).then_inc(bank_free, 1)
                            g += 1

            def empty_group(tiles, place):
                dve.wait_ge(lo_slot_free, tiles + LO)
                for t in range(TT):
                    for ch in range(NCH):
                        place(U[:, t * NCH + ch], t, slice(ch * 512, (ch + 1) * 512)).then_inc(bank_free, 1)

            def conv_tap(g, n):
                a, shift = n % 2, n // 2
                ct = 2 * g + a
                weight = taps[:, ct, TAPS - 1 - shift:TAPS - shift]
                if shift == 0:
                    nc.vector.tensor_scalar(conv_out[:, ct, :], conv_in[:, ct, :], weight, b_dw_col(g, a),
                                            ALU.mult, ALU.add).then_inc(conv_step, 1)
                else:
                    dve.wait_ge(conv_step, 2 * TAPS * g + n - 1)
                    nc.vector.scalar_tensor_tensor(out=conv_out[:, ct, shift:T], in0=conv_in[:, ct, 0:T - shift],
                                                   scalar=weight, in1=conv_out[:, ct, shift:T],
                                                   op0=ALU.mult, op1=ALU.add).then_inc(conv_step, 1)

            def b_dw_col(g, a):
                return cols2[:, bass.ds(2 * CT + 2 * g + a, 1)]

            def prepare_pair(step, p):
                if step == "mean":
                    dve.wait_ge(sq_ready, 8 * (p + 1))
                    nc.vector.tensor_scalar(hstat[:, 0], hstat[:, 0], 1.0 / HD, EPS, ALU.mult, ALU.add).then_inc(hstat_dve, 1)
                if step == "newton":
                    dve.wait_ge(hstat_act, 2 * (p + 1))
                    nc.vector.tensor_tensor(hstat[:, 2], hstat[:, 1], hstat[:, 1], ALU.mult).then_inc(hstat_dve, 1)
                    dve.wait_ge(hstat_dve, 4 * p + 2)
                    nc.vector.tensor_tensor(hstat[:, 2], hstat[:, 2], hstat[:, 0], ALU.mult).then_inc(hstat_dve, 1)
                    dve.wait_ge(hstat_dve, 4 * p + 3)
                    nc.vector.tensor_scalar(hstat[:, 2], hstat[:, 2], -0.5, 1.5, ALU.mult, ALU.add).then_inc(hstat_dve, 1)
                    dve.wait_ge(hstat_dve, 4 * p + 4)
                    nc.vector.tensor_tensor(hstat[:, 2], hstat[:, 2], hstat[:, 1], ALU.mult).then_inc(hstat_ready, 1)
                if step == "gate":
                    dve.wait_ge(eg_ready, p + 1)
                    nc.vector.tensor_scalar(sig[:], sig[:], 1.0, None, ALU.add).then_inc(sig_step, 1)
                    dve.wait_ge(sig_step, 3 * p + 1)
                    nc.vector.reciprocal(sig[:], sig[:]).then_inc(sig_step, 1)
                    dve.wait_ge(sig_step, 3 * p + 2)
                    nc.vector.tensor_tensor(sig[:], sig[:], pair[:, :, 6 * HD:8 * HD], ALU.mult).then_inc(sig_step, 1)

            def attend(step, p, local):
                h = 2 * p + local
                if step == "soft":
                    dve.wait_ge(log_ready, h + 1)
                    nc.vector.scalar_tensor_tensor(out=absz, in0=X[1][:, 0:3 * P], scalar=0.0, in1=absz,
                                                   op0=ALU.max, op1=ALU.add).then_inc(soft_ready, 1)
                if step == "y":
                    dve.wait_ge(o_ps, ONE + h + 1)
                    dve.wait_ge(sig_step, 3 * p + 3)
                    nc.vector.tensor_tensor(ysb[:, :, bass.ds(h * HD, HD)], X[2][:, 0:T].rearrange("p (t d) -> p t d", t=TT),
                                            sig[:, :, local * HD:(local + 1) * HD], ALU.mult).then_inc(y_done, 1)

            DVE_PREP = {3: "mean", 4: "newton", 5: "gate"}
            DVE_STEPS = {14: ("soft", 0), 19: ("y", 0), 23: ("soft", 1), 28: ("y", 1)}
            CONV_STEPS = 2 * TAPS

            def keep_pair(bank, t, columns):
                return nc.vector.tensor_copy(pair[:, t, columns], bank)

            def split_pair_tile(g, k):
                low(TILE_B + g * KT + k, k, k // 2 % SLOTS, k % 2)

            for k in range(KT):
                split_pair_tile(0, k)
                if k == 0:
                    dve.wait_ge(bank_free, 4 * GROUP_B + 4)
                if 1 <= k <= 4:
                    n = k - 1
                    dve.wait_ge(gates_ready, n + 1)
                    u, gate = ubuf[:, n // 2, n % 2], glubuf[:, n // 2, n % 2]
                    nc.vector.tensor_tensor(u, u, gate, ALU.mult).then_inc(glu_ready, 1)
                if k >= KT // 2:
                    if k == KT // 2:
                        dve.wait_ge(gluT_sb, CT // 2)
                    for n in range(4 * (k - KT // 2), min(4 * (k - KT // 2) + 4, CONV_STEPS)):
                        conv_tap(0, n)
            empty_group(TILE_B + KT, keep_pair)
            with dve.Fori(1, PAIRS) as g:
                n = 0
                for k in range(KT):
                    split_pair_tile(g, k)
                    if k in DVE_PREP:
                        prepare_pair(DVE_PREP[k], g - 1)
                    if k in DVE_STEPS:
                        attend(DVE_STEPS[k][0], g - 1, DVE_STEPS[k][1])
                    for _ in range(2 if 6 <= k < KT - 3 else 0):
                        conv_tap(g, n)
                        n += 1
                while n < CONV_STEPS:
                    conv_tap(g, n)
                    n += 1
                empty_group(TILE_B + g * KT + KT, keep_pair)

            p = PAIRS - 1
            for step in ("mean", "newton", "gate"):
                prepare_pair(step, p)
            dve.wait_ge(mean_ps, 1)
            nc.vector.tensor_scalar(ln_stat[:], X[0][:, 0:T], 1.0 / CW, None, ALU.mult).then_inc(xc_ready, 1)
            attend("soft", p, 0)
            dve.wait_ge(xc_ready, 1)
            across = ln_stat[:].unsqueeze(1).to_broadcast([P, 4, T])
            for n in range(4):
                part = conv_out[:, 4 * n:4 * n + 4]
                nc.vector.tensor_tensor(part, part, across, ALU.add).then_inc(xc_ready, 1)
            attend("y", p, 0)
            attend("soft", p, 1)
            dve.wait_ge(var_ps, 1)
            nc.vector.tensor_scalar(ln_stat[:], X[0][:, 0:T], 1.0 / CW, EPS, ALU.mult, ALU.add).then_inc(var_ready, 1)
            attend("y", p, 1)
            dve.wait_ge(deviation_ready, 1)
            then(nc.vector.reciprocal(ln_stat[:], ln_stat[:]))
            dve.wait_ge(sqc_ready, 4)
            for n in range(4):
                part = conv_out[:, 4 * n:4 * n + 4]
                nc.vector.tensor_tensor(part, part, across, ALU.mult).then_inc(norm_ready, 1)
            for r in range(CT // 2):
                dve.wait_ge(conv_hi, r + 1)
                two = slice(2 * r, 2 * r + 2)
                nc.vector.tensor_tensor(act_lo[:, two], conv_out[:, two], act_hi[:, two].bitcast(F32),
                                        ALU.subtract).then_inc(conv_lo, 1)

            def y_low(r, high_ready, ready, tile):
                dve.wait_ge(high_ready, r + 1)
                two = slice(tile, tile + 2)
                nc.vector.tensor_tensor(act_lo[:, two].rearrange("p c t -> p (c t)"), X[r % 2][:],
                                        act_hi[:, two].bitcast(F32).rearrange("p c t -> p (c t)"),
                                        ALU.subtract).then_inc(ready, 1)

            for s in range(PG * PKT):
                low(TILE_P + s, s, s // 2 % SLOTS, s % 2)
                if s >= 7 and s % 2 == 1 and s < 7 + CT:
                    r = (s - 7) // 2
                    y_low(r, ysb_hi, ysb_lo, KT // 2 + 2 * r)
                if s % PKT == PKT - 1:
                    gates = gatebuf[:, s // PKT]
                    empty_group(TILE_P + s + 1, lambda bank, t, columns: nc.vector.tensor_tensor(
                        gates[:, t, columns], gates[:, t, columns], bank, ALU.mult))
            for r in range(CT // 2):
                y_low(r, yc_hi, yc_lo, 2 * r)

            with dve.Fori(0, OG) as g:
                for n in range(KT):
                    if n % 2 == 0:
                        dve.wait_ge(raw_landed[n % SLOTS], landed(ITEM_O + n) + EXTRA + g * (KT // SLOTS * 16))
                        if n == 0:
                            dve.wait_ge(gate_ps, ONE + g)
                            nc.vector.tensor_scalar(gate_sum, raw[:, 0, 0], silu_c[:, 0:1], None, ALU.mult).then_inc(gate_step, 1)
                        else:
                            dve.wait_ge(item_summed, SUM_O + g * (KT // 2) + n // 2)
                            nc.vector.scalar_tensor_tensor(out=gate_sum, in0=raw[:, n % SLOTS, 0], scalar=silu_c[:, n:n + 1],
                                                           in1=gate_sum, op0=ALU.mult, op1=ALU.add).then_inc(gate_step, 1)
                        dve.wait_ge(gate_step, g * (KT // 2) + n // 2 + 1)
                        nc.vector.scalar_tensor_tensor(out=gate_sum, in0=raw[:, n % SLOTS, 1], scalar=silu_c[:, n + 1:n + 2],
                                                       in1=gate_sum, op0=ALU.mult, op1=ALU.add).then_inc(item_summed, 1)
                    else:
                        for kk in range(2):
                            k = n - 1 + kk
                            low(TILE_O + g * KT + k, k, n % SLOTS, kk)
                dve.wait_ge(gate_ready, ONE + 2 * g + 2)
                dve.wait_ge(y_out_free, ONE + g)
                empty_group(TILE_O + g * KT + KT, lambda bank, t, columns: nc.vector.tensor_tensor(
                    y_out[:, t, columns], bank, gate_sb[:, columns], ALU.mult))
                dve.wait_ge(xres_landed, 16 * g + 16)
                dve.wait_ge(bank_free, 4 * (GROUP_O + g + 1) + 4)
                nc.vector.tensor_tensor(y_out, y_out, x_res, ALU.add).then_inc(out_ready, 1)


_INS = ["x", "c", "norm_g", "w_ada", "b_ada", "w_in", "q_norm_g", "k_norm_g", "w_dw", "b_dw", "ln_g", "ln_b",
        "w_pw", "b_pw", "w_out"]


def kernel(**inputs):
    import concourse.bacc as bacc
    from concourse.bass_utils import run_bass_kernel_spmd

    nc = bacc.Bacc("TRN2", target_bir_lowering=False, num_devices=1)
    arrays, args = {}, []
    for name in _INS:
        a = np.ascontiguousarray(inputs[name])
        arrays[f"in_{name}"] = a
        args.append(nc.dram_tensor(f"in_{name}", a.shape, mybir.dt.from_np(a.dtype), kind="ExternalInput").ap())
    out = nc.dram_tensor("out_x", (1, T, D), F32, kind="ExternalOutput").ap()
    hybrid_layer(nc, *args, out)
    r = run_bass_kernel_spmd(nc, [arrays], core_ids=[0])
    return r.results[0]["out_x"]
```

```python
import numpy as np
from contextlib import ExitStack

import concourse.bass as bass
from concourse import mybir

F32 = mybir.dt.float32
BF16 = mybir.dt.bfloat16
F32R = mybir.dt.float32r
ACT = mybir.ActivationFunctionType
ALU = mybir.AluOpType

P = 128
D = 4096
T = 256
TT = T // P
HD = 128
SBW = D // 2
CW = D - SBW
TAPS = 31
EPS = 1e-6
NEVER = -2.0 ** 100
ONE = 1
KT = D // P
GC = 1024
NCH = GC // 512
BK = 8
NB = KT // BK
AG = 3 * CW // GC
PAIRS = SBW // (2 * HD)
PG = CW // GC
PKT = CW // P
OG = D // GC
CT = CW // P
SLOTS = 4
HI = 4
LO = 2

BODY = ("w", "a", "w", "a", "a", "w", "a", "a", "w", "a", "e") * 2
END = ("w", "a", "w", "a", "a", "w", "a", "w", "a", "e", "w", "a", "w", "a", "a", "w", "w", "e")
LAST_BODY = ("w", "a", "w", "a", "w", "w", "e", "w", "a", "w", "w", "a", "w", "e")
LAST_END = ("w", "a", "w", "a", "w", "a", "w", "e", "a", "w", "a", "w", "a", "w", "a", "w", "a", "e")
P_ITEMS = ("a",) * 4 + ("w", "a", "w", "a", "w", "a", "w") * 3 + ("a",) * 3 + ("w",) * 4
O_BODY = ("w", "a", "w") * 8 + ("w", "a", "w", "a", "w") * 4 + ("w",) * 4
TAIL_ITEMS = 4
GATE_ITEMS = 16
GROUPS_PER_BODY = 2
BODIES = AG // GROUPS_PER_BODY - 1

ITEM_ADA0 = 4
ITEM_A = ITEM_ADA0 + KT
BODY_ITEMS = BODY.count("w") + BODY.count("a")
A_PER_BODY = BODY.count("a")
BLOCK_ITEMS = BODIES * BODY_ITEMS + END.count("w") + END.count("a")
LAST_ITEMS = BODIES * (LAST_BODY.count("w") + LAST_BODY.count("a")) + LAST_END.count("w") + LAST_END.count("a")
ITEM_B = ITEM_A + (NB - 1) * BLOCK_ITEMS + LAST_ITEMS
ITEM_P = ITEM_B + PAIRS * KT // 2
ITEM_O = ITEM_P + len(P_ITEMS)
SUM_A = 4 + KT
SUM_LAST = 4 + NB * KT
SUM_P = SUM_LAST + GATE_ITEMS
SUM_O = SUM_P + GATE_ITEMS
TILE_B = AG * KT
TILE_P = TILE_B + PAIRS * KT
TILE_O = TILE_P + PG * PKT
GROUP_B = AG * NB
GROUP_P = GROUP_B + PAIRS
GROUP_O = GROUP_P + PG

GCOL_TILE = 24


def held(tail, kinds, n):
    history = tail + kinds
    return history[n], history[SLOTS:n + 1].count(history[n]) if n >= SLOTS else -history[n + 1:SLOTS].count(history[n])


def items_of(body):
    return [kind for kind in body if kind != "e"]


def hybrid_layer(nc, x, c, norm_g, w_ada, b_ada, w_in, q_norm_g, k_norm_g,
                 w_dw, b_dw, ln_g, ln_b, w_pw, b_pw, w_out, out):
    x_rows = x[0].rearrange("(t p) n -> p t n", p=P)
    out_rows = out[0].rearrange("(t p) (g n) -> g p t n", p=P, n=GC)
    ada_rows = w_ada[0].rearrange("(k p) (s b n) -> k p s b n", p=P, s=3, b=NB)
    gate_pairs = w_ada[0][:, 2 * D:3 * D].rearrange("(k two p) (g n) -> k p g two n", p=P, two=2, n=GC)
    conv_rows = w_in[0][:, 4 * SBW:].rearrange("(k p) (g n) -> g p k n", p=P, n=GC)
    pair_rows = w_in[0][:, 0:4 * SBW].rearrange("(k p) (r g n) -> g k p r n", p=P, r=4, n=2 * HD)
    pw_rows = w_pw[0].rearrange("(k p) (g n) -> g p k n", p=P, n=GC)
    wo_rows = w_out[0].rearrange("(k p) (g n) -> g p k n", p=P, n=GC)

    ctx = ExitStack()
    with ctx:
        def sb(name, shape, dt=F32):
            return ctx.enter_context(nc.sbuf_tensor(name, shape, dt))

        def bank(name, shape):
            return ctx.enter_context(nc.psum_tensor(name, shape, F32))

        def sem(name):
            return ctx.enter_context(nc.semaphore(name))

        act_hi = sb("act_hi", [P, KT, T], F32R)
        act_lo = sb("act_lo", [P, KT, T], F32R)
        raw = sb("raw", [P, SLOTS, 2, GC])
        whi = sb("whi", [P, HI, GC], F32R)
        wlo = sb("wlo", [P, LO, GC], F32R)
        cbuf = sb("cbuf", [P, AG, TT, GC])
        wide = sb("wide", [P, 2 * GC])
        ysb = sb("ysb", [P, TT, SBW])
        tmp = sb("tmp", [P, 2, 2, T])
        wexp = sb("wexp", [P, 3 * P])
        ident = sb("ident", [P, P])
        neg_tri = sb("neg_tri", [P, P])
        neg_ones = sb("neg_ones", [P, P])
        ones = sb("ones", [P, P])
        never = sb("never", [P, P], BF16)
        ident_b = sb("ident_b", [P, P], BF16)
        cols = sb("cols", [P, 4, KT])
        cols2 = sb("cols2", [P, 3 * CT + 2 + KT])
        gate_cols = sb("gate_cols", [P, OG, GC // P])
        taps = sb("taps", [P, CT, TAPS])
        silu_c = sb("silu_c", [P, KT])
        xstat = sb("xstat", [P, 12])
        mod_mul = sb("mod_mul", [P, BK])
        mod_add = sb("mod_add", [P, BK])
        hstat = sb("hstat", [P, 3, 8])
        sig = sb("sig", [P, TT, 2 * HD])
        ln_stat = sb("ln_stat", [P, T])
        ubuf, glubuf, gatebuf = cbuf[:, 0:2], cbuf[:, 2:4], cbuf[:, 4:6]

        x_block = ysb[:].rearrange("p b (t n) -> p b t n", t=TT)
        h32 = tmp
        qkT = tmp[:, 0]
        absz = tmp[:, 1].rearrange("p a t -> p (a t)")[:, 0:3 * P]
        pair = wide[:].rearrange("p (t n) -> p t n", t=TT)
        conv_in = glubuf.rearrange("p a t n -> p (a t n)").rearrange("p (c t) -> p c t", t=T)
        conv_out = ubuf.rearrange("p a t n -> p (a t n)").rearrange("p (c t) -> p c t", t=T)
        squares = tmp[:].rearrange("p a b (c n) -> p (a b c) n", n=P)
        gate_sum0 = wide[:, 0:GC]
        gate_sum = cbuf[:, 3, 0]
        gate_diag = cbuf[:, 3, 1].rearrange("p (j n) -> p j n", n=P)
        gate_sb = tmp[:].rearrange("p a b t -> p (a b t)")
        x_res = cbuf[:, 0]
        y_out = cbuf[:, 2]
        param_rows = raw[:, SLOTS - 1, 0, 0:P]
        param_rows2 = raw[:, SLOTS - 1, 0, P:2 * P]
        tap_rows = cbuf[:, 2].rearrange("p t n -> p (t n)")

        U = bank("U", [P, 4, 512])
        X = [bank(f"X{i}", [P, 512]) for i in range(4)]

        raw_landed = [sem(f"raw_landed{i}") for i in range(SLOTS)]
        params_landed, taps_landed = sem("params_landed"), sem("taps_landed")
        x_landed = [sem("x_landed0"), sem("x_landed1")]
        xres_landed = sem("xres_landed")
        bpw_landed, stored = sem("bpw_landed"), sem("stored")
        item_summed = sem("item_summed")
        hi_ready, lo_ready = sem("hi_ready"), sem("lo_ready")
        hi_slot_free, lo_slot_free = sem("hi_slot_free"), sem("lo_slot_free")
        bank_free, half_done = sem("bank_free"), sem("half_done")
        consts_ready, pool_step = sem("consts_ready"), sem("pool_step")
        params_ps, params_sb, silu_ready = sem("params_ps"), sem("params_sb"), sem("silu_ready")
        ms_ready, rms_ready, rstd_ready = sem("ms_ready"), sem("rms_ready"), sem("rstd_ready")
        dve_step = sem("dve_step")
        mod_summed, wide_zeroed, mod_ready = sem("mod_summed"), sem("wide_zeroed"), sem("mod_ready")
        x_scaled, xT_ps, h_ready = sem("x_scaled"), sem("xT_ps"), sem("h_ready")
        act_hi_ready, act_lo_ready = sem("act_hi_ready"), sem("act_lo_ready")
        gates_ready, glu_ready, gluT_ps, gluT_sb = sem("gates_ready"), sem("glu_ready"), sem("gluT_ps"), sem("gluT_sb")
        conv_step = sem("conv_step")
        sq_ready, hstat_act, hstat_dve, hstat_ready = sem("sq_ready"), sem("hstat_act"), sem("hstat_dve"), sem("hstat_ready")
        sig_ready, qk_scaled = sem("sig_ready"), sem("qk_scaled")
        qkT_ps, qkT_sb, z_ps, abs_ready = sem("qkT_ps"), sem("qkT_sb"), sem("z_ps"), sem("abs_ready")
        exp_ready, log_ready, soft_step, soft_ready = sem("exp_ready"), sem("log_ready"), sem("soft_step"), sem("soft_ready")
        logw_ps, w_ready, o_ps, y_done = sem("logw_ps"), sem("w_ready"), sem("o_ps"), sem("y_done")
        mean_ps, xc_ready, sqc_ready, var_ps = sem("mean_ps"), sem("xc_ready"), sem("sqc_ready"), sem("var_ps")
        var_ready, deviation_ready = sem("var_ready"), sem("deviation_ready")
        norm_ready, swish_ready = sem("norm_ready"), sem("swish_ready")
        conv_hi, conv_lo = sem("conv_hi"), sem("conv_lo")
        ysbT_ps, ysb_hi, ysb_lo = sem("ysbT_ps"), sem("ysb_hi"), sem("ysb_lo")
        ycT_ps, yc_hi, yc_lo = sem("ycT_ps"), sem("yc_hi"), sem("yc_lo")
        gate_step, gate_zeroed, gcol_ps, gcol_ready = sem("gate_step"), sem("gate_zeroed"), sem("gcol_ps"), sem("gcol_ready")
        diag_ready, gate_ps, gate_ready = sem("diag_ready"), sem("gate_ps"), sem("gate_ready")
        out_ready, y_out_free = sem("out_ready"), sem("y_out_free")

        block = ctx.enter_context(nc.Block())

        @block.sync
        def _(sp):
            def load(slot, dst, src, summed=None, split=None):
                if summed is not None:
                    sp.wait_ge(item_summed, summed)
                if split is not None:
                    if not isinstance(split, int):
                        split = sp.snap(split)
                        sp.wait_ge(params_ps, 1)
                    sp.wait_ge(lo_ready, split)
                sp.dma_start(dst, src).then_inc(raw_landed[slot], 16)

            def load_x(b):
                if b >= 2:
                    sp.wait_ge(xT_ps, BK // 2 * (b - 1))
                sp.dma_start(x_block[:, b % 2], x_rows[:, :, b * BK * P:(b + 1) * BK * P]).then_inc(x_landed[b % 2], 16)

            for n in range(SLOTS):
                if n == SLOTS - 1:
                    sp.wait_ge(params_ps, 1)
                sp.dma_start(raw[:, n].rearrange("p a n -> p (a n)"),
                             x_rows[:, n // 2, n % 2 * 2 * GC:(n % 2 + 1) * 2 * GC]).then_inc(raw_landed[n], 16)
            for k in range(KT):
                n = ITEM_ADA0 + k
                load(n % SLOTS, raw[:, n % SLOTS], ada_rows[k, :, 0:2, 0, :], summed=n - SLOTS + 1)
                if k == 8:
                    load_x(0)
                if k == 16:
                    load_x(1)
            def wait_of(tail, kinds, n, tiles, sums):
                kind, number = held(tail, kinds, n)
                return dict(summed=sums + number) if kind == "a" else dict(split=tiles + 2 * number)

            tail = ["a"] * SLOTS
            for b in range(NB):
                body, end = (items_of(LAST_BODY), items_of(LAST_END)) if b == NB - 1 else (items_of(BODY), items_of(END))
                sums = SUM_A + KT * b

                def load_item(n, it):
                    wait = wait_of(tail, body + end, n, BK * AG * b + it * (BK * GROUPS_PER_BODY),
                                   sums + it * body.count("a"))
                    kinds = body + end
                    w, a, slot = kinds[:n].count("w"), kinds[:n].count("a") + it * body.count("a"), n % SLOTS
                    if kinds[n] == "w":
                        g, k0 = w // (BK // 2), b * BK + 2 * (w % (BK // 2))
                        load(slot, raw[:, slot], conv_rows[it * GROUPS_PER_BODY + g, :, k0:k0 + 2, :], **wait)
                    elif b < NB - 1:
                        load(slot, raw[:, slot], ada_rows[a, :, 0:2, b + 1, :], **wait)
                    else:
                        load(slot, raw[:, slot], gate_pairs[a, :, 0], **wait)

                if b in (1, 2):
                    load_x(b + 1)
                for n in range(SLOTS):
                    load_item(n, 0)
                with sp.Fori(0, BODIES) as it:
                    for n in range(SLOTS, len(body) + SLOTS):
                        load_item(n, it)
                for n in range(len(body) + SLOTS, len(body) + len(end)):
                    load_item(n, BODIES - 1)
                tail = end[-SLOTS:]

            def load_pair(g, tail):
                for kp in range(KT // 2):
                    kind, number = held(tail, ["w"] * (KT // 2), kp)
                    if kind == "a":
                        sp.wait_ge(item_summed, SUM_P + number)
                    else:
                        sp.wait_ge(lo_ready, TILE_B + g * KT + 2 * number)
                    for kk in range(2):
                        sp.dma_start(raw[:, kp % SLOTS, kk].rearrange("p (r n) -> p r n", r=4),
                                     pair_rows[g, 2 * kp + kk]).then_inc(raw_landed[kp % SLOTS], 16)

            ALL_WEIGHTS = ["w"] * SLOTS
            load_pair(0, tail)
            with sp.Fori(1, PAIRS) as g:
                load_pair(g, ALL_WEIGHTS)
            w_items = a_items = 0
            for n, kind in enumerate(P_ITEMS):
                wait = wait_of(ALL_WEIGHTS, list(P_ITEMS), n, TILE_P, SUM_P)
                if kind == "w":
                    g, k0 = w_items // (PKT // 2), 2 * (w_items % (PKT // 2))
                    load(n % SLOTS, raw[:, n % SLOTS], pw_rows[g, :, k0:k0 + 2, :], **wait)
                    w_items += 1
                else:
                    load(n % SLOTS, raw[:, n % SLOTS], gate_pairs[a_items, :, 1], **wait)
                    a_items += 1
            with sp.Fori(0, OG // 2) as it:
                w_items = a_items = 0
                for n, kind in enumerate(O_BODY):
                    wait = wait_of(ALL_WEIGHTS, list(O_BODY), n, TILE_O + it * (2 * KT), SUM_O + it * GATE_ITEMS)
                    if kind == "w":
                        g, k0 = w_items // (KT // 2), 2 * (w_items % (KT // 2))
                        load(n % SLOTS, raw[:, n % SLOTS], wo_rows[it * 2 + g, :, k0:k0 + 2, :], **wait)
                        w_items += 1
                    else:
                        load(n % SLOTS, raw[:, n % SLOTS], gate_pairs[a_items, :, it + 2], **wait)
                        a_items += 1

        def landed(item):
            return 16 * (item // SLOTS + 1)

        def landed_b(g, kp):
            return 16 * (ITEM_B // SLOTS) + (KT // 2 // SLOTS) * 32 * g + 32 * (kp // SLOTS + 1)

        EXTRA = 16 * (PAIRS * KT // 2 // SLOTS)

        @block.tensor
        def _(pe):
            pe.sem_inc(hi_slot_free, HI)
            pe.sem_inc(lo_slot_free, LO)
            for s in (z_ps, logw_ps, o_ps, gate_ps):
                pe.sem_inc(s, ONE)

            def k_tile(tile, count, slot, group=None, first=False, last=False, seeded=False):
                hi, lo = whi[:, slot % HI], wlo[:, slot % LO]
                pe.wait_ge(hi_ready, count + 1)
                if last:
                    pe.wait_ge(lo_ready, count + 1)
                    for t in range(TT):
                        for part, weights in ((act_hi, hi), (act_lo, hi), (act_hi, lo)):
                            for ch in range(NCH):
                                m = nc.tensor.matmul(U[:, t * NCH + ch], part[:, tile, t * P:(t + 1) * P],
                                                     weights[:, ch * 512:(ch + 1) * 512],
                                                     start=False, stop=weights is lo)
                                if t == TT - 1 and weights is lo and ch == 0:
                                    m.then_inc(hi_slot_free, 1)
                        m.then_inc(lo_slot_free if t == TT - 1 else half_done, 1)
                    return
                for t in range(TT):
                    for part in (act_hi, act_lo):
                        for ch in range(NCH):
                            if first and not seeded and part is act_hi:
                                pe.wait_ge(bank_free, 4 * group + t * NCH + ch + 1)
                            nc.tensor.matmul(U[:, t * NCH + ch], part[:, tile, t * P:(t + 1) * P],
                                             hi[:, ch * 512:(ch + 1) * 512],
                                             start=first and not seeded and part is act_hi, stop=False)
                pe.wait_ge(lo_ready, count + 1)
                for t in range(TT):
                    for ch in range(NCH):
                        m = nc.tensor.matmul(U[:, t * NCH + ch], act_hi[:, tile, t * P:(t + 1) * P],
                                             lo[:, ch * 512:(ch + 1) * 512], start=False, stop=False)
                        if t == 0 and ch == 0:
                            m.then_inc(hi_slot_free, 1)
                m.then_inc(lo_slot_free, 1)

            pe.wait_ge(consts_ready, 1)
            pe.wait_ge(params_landed, 16 * 10)
            nc.tensor.transpose(X[0][:, 0:P], param_rows, ident[:])
            nc.tensor.transpose(X[0][:, P:2 * P], param_rows2, ident[:]).then_inc(params_ps, 1)
            pe.wait_ge(taps_landed, 16)
            for ct in range(CT):
                m = nc.tensor.transpose(X[1][:, ct * TAPS:(ct + 1) * TAPS], tap_rows[0:TAPS, ct * P:(ct + 1) * P],
                                        ident[0:TAPS, 0:TAPS])
            m.then_inc(params_ps, 1)
            pe.wait_ge(params_sb, 2)

            def mod_sums(b):
                pe.wait_ge(item_summed, 4 + KT * (b + 1))
                for s in range(2):
                    for j in range(BK):
                        m = nc.tensor.matmul(X[3][:, s * BK + j:s * BK + j + 1],
                                             wide[:, s * GC + j * P:s * GC + (j + 1) * P], ones[:, 0:1],
                                             start=True, stop=True)
                m.then_inc(mod_summed, 1)

            def x_transpose(b, q):
                if q == 0:
                    pe.wait_ge(x_scaled, 2 * (b + 1))
                if q == 3:
                    pe.wait_ge(h_ready, b * (BK // 2) + 1)
                for kk in range(2):
                    for t in range(TT):
                        k = 2 * q + kk
                        m = nc.tensor.transpose(X[q % 3][:, kk * T + t * P:kk * T + (t + 1) * P],
                                                x_block[:, b % 2, t, k * P:(k + 1) * P], ident[:])
                m.then_inc(xT_ps, 1)

            def two_groups(b, it, after):
                for k in range(GROUPS_PER_BODY * BK):
                    k_tile(b * BK + k % BK, AG * BK * b + it * (GROUPS_PER_BODY * BK) + k, k,
                           AG * b + it * GROUPS_PER_BODY + k // BK, first=k % BK == 0, last=k % BK == BK - 1)
                    for step, *which in after.get(k, ()):
                        step(b + 1, *which)

            for q in range(3):
                x_transpose(0, q)
            mod_sums(0)
            x_transpose(0, 3)
            for b in range(NB):
                pe.wait_ge(act_lo_ready, (b + 1) * (BK // 2))
                pe.wait_ge(act_hi_ready, (b + 1) * (BK // 2))
                with pe.Fori(0, BODIES) as it:
                    two_groups(b, it, {})
                two_groups(b, BODIES, {} if b == NB - 1 else {
                    9: [(x_transpose, 0)], 10: [(x_transpose, 1)], 11: [(x_transpose, 2), (mod_sums,)],
                    13: [(x_transpose, 3)]})

            def gate_columns(n, ps, sums):
                pe.wait_ge(item_summed, SUM_LAST + GATE_ITEMS * (n + 1))
                for j in range(GC // P):
                    m = nc.tensor.matmul(ps[:, j:j + 1], sums[:, j * P:(j + 1) * P], ones[:, 0:1], start=True, stop=True)
                m.then_inc(gcol_ps, 1)

            def glu_transpose(r):
                if r == 0:
                    pe.wait_ge(glu_ready, 4)
                if r >= 2:
                    pe.wait_ge(gluT_sb, r - 1)
                for kk in range(2):
                    ct = 2 * r + kk
                    for t in range(TT):
                        m = nc.tensor.transpose(X[r % 2][:, kk * T + t * P:kk * T + (t + 1) * P],
                                                ubuf[:, ct // 8, t, ct % 8 * P:(ct % 8 + 1) * P], ident[:])
                m.then_inc(gluT_ps, 1)

            def attend(step, h, local):
                if step == "transpose":
                    pe.wait_ge(qk_scaled, h + 1)
                    pe.wait_ge(qkT_sb, ONE + h)
                    for s in range(2):
                        for t in range(TT):
                            m = nc.tensor.transpose(X[3][:, s * T + t * P:s * T + (t + 1) * P],
                                                    pair[:, t, (2 * s + local) * HD:(2 * s + local + 1) * HD], ident[:])
                    m.then_inc(qkT_ps, 1)
                if step == "z":
                    pe.wait_ge(qkT_sb, ONE + h + 1)
                    pe.wait_ge(w_ready, ONE + h)
                    nc.tensor.matmul(X[1][:, 0:T], qkT[:, 1, 0:P], qkT[:, 0, :], start=True, stop=False,
                                     skip_group_check=True)
                    nc.tensor.matmul(X[1][:, T:T + P], qkT[:, 1, P:T], qkT[:, 0, P:T], start=False, stop=False,
                                     skip_group_check=True)
                    for diagonal in (0, T):
                        m = nc.tensor.matmul(X[1][:, diagonal:diagonal + P], ident_b[:], never[:], start=False,
                                             stop=False, skip_group_check=True)
                    m.then_inc(z_ps, 1)
                if step == "sum":
                    pe.wait_ge(soft_ready, h + 1)
                    nc.tensor.matmul(X[1][:, 0:T], neg_tri[:], absz[:, 0:T], start=False, stop=False,
                                     skip_group_check=True)
                    nc.tensor.matmul(X[1][:, P:T], neg_ones[:], absz[:, T:T + P], start=False, stop=False,
                                     skip_group_check=True)
                    nc.tensor.matmul(X[1][:, T:T + P], neg_tri[:], absz[:, T:T + P], start=False, stop=True,
                                     skip_group_check=True).then_inc(logw_ps, 1)
                if step == "o":
                    v = (4 + local) * HD
                    pe.wait_ge(w_ready, ONE + h + 1)
                    pe.wait_ge(y_done, ONE + h)
                    nc.tensor.matmul(X[2][:, 0:P], wexp[:, 0:P], pair[:, 0, v:v + HD], start=True, stop=True)
                    nc.tensor.matmul(X[2][:, P:T], wexp[:, P:T], pair[:, 0, v:v + HD], start=False, stop=False,
                                     skip_group_check=True)
                    nc.tensor.matmul(X[2][:, P:T], wexp[:, T:T + P], pair[:, 1, v:v + HD], start=False, stop=True,
                                     skip_group_check=True).then_inc(o_ps, 1)

            PE_STEPS = {8: ("transpose", 0), 10: ("z", 0), 14: ("sum", 0), 16: ("transpose", 1), 17: ("o", 0),
                        19: ("z", 1), 23: ("sum", 1), 26: ("o", 1)}
            for k in range(KT):
                k_tile(k, TILE_B + k, k, GROUP_B, first=k == 0, last=k == KT - 1)
                if 4 <= k < 4 + CT // 2:
                    glu_transpose(k - 4)
                if k == 3:
                    gate_columns(0, X[3], gate_sum0)
            pe.wait_ge(gcol_ready, 1)
            with pe.Fori(1, PAIRS) as g:
                for k in range(KT):
                    k_tile(k, TILE_B + g * KT + k, k, GROUP_B + g, first=k == 0, last=k == KT - 1)
                    if k in PE_STEPS:
                        step, local = PE_STEPS[k]
                        attend(step, (g - 1) * 2 + local, local)

            last = 2 * (PAIRS - 1)
            attend("transpose", last, 0)
            attend("z", last, 0)
            pe.wait_ge(conv_step, CT * TAPS)
            pe.wait_ge(gluT_sb, CT // 2)
            for ct in range(CT):
                m = nc.tensor.matmul(X[0][:, 0:T], neg_ones[:], conv_out[:, ct], start=ct == 0, stop=ct == CT - 1)
            m.then_inc(mean_ps, 1)
            attend("sum", last, 0)
            attend("transpose", last + 1, 1)
            attend("o", last, 0)
            attend("z", last + 1, 1)
            for ct in range(CT):
                if ct % 4 == 0:
                    pe.wait_ge(sqc_ready, ct // 4 + 1)
                    if ct == 0:
                        pe.wait_ge(xc_ready, 1)
                m = nc.tensor.matmul(X[0][:, 0:T], ones[:], conv_in[:, ct], start=ct == 0, stop=ct == CT - 1)
            m.then_inc(var_ps, 1)
            attend("sum", last + 1, 1)
            attend("o", last + 1, 1)

            def y_transpose(r, source, seen, free, ready):
                pe.wait_ge(seen[0], seen[1])
                if r >= 2:
                    pe.wait_ge(free, r - 1)
                for kk in range(2):
                    for t in range(TT):
                        m = nc.tensor.transpose(X[r % 2][:, kk * T + t * P:kk * T + (t + 1) * P],
                                                source(2 * r + kk, t), ident[:])
                m.then_inc(ready, 1)

            pe.wait_ge(bpw_landed, 16)
            pe.wait_ge(var_ready, 1)
            for g in range(PG):
                for t in range(TT):
                    for ch in range(NCH):
                        pe.wait_ge(bank_free, 4 * (GROUP_P + g) + t * NCH + ch + 1)
                        nc.tensor.matmul(U[:, t * NCH + ch], ones[0:1, :],
                                         wide[0:1, g * GC + ch * 512:g * GC + (ch + 1) * 512], start=True, stop=False)
                for k in range(PKT):
                    if g == 0:
                        pe.wait_ge(conv_lo, k // 2 + 1)
                    k_tile(k, TILE_P + g * PKT + k, k, last=k == PKT - 1, first=k == 0, seeded=True)
                    s = g * PKT + k
                    if s >= 4 and s % 2 == 0 and s < 4 + CT:
                        r = (s - 4) // 2
                        y_transpose(r, lambda kt, t: ysb[:, t, kt * P:(kt + 1) * P], (y_done, ONE + 2 * PAIRS), ysb_lo, ysbT_ps)
                    if s == PG * PKT - 4:
                        gate_columns(1, X[3], gate_sum)

            pe.wait_ge(ysb_lo, CT // 2)
            for r in range(CT // 2):
                y_transpose(r, lambda kt, t: gatebuf[:, kt // 8, t, kt % 8 * P:(kt % 8 + 1) * P],
                            (bank_free, 4 * (GROUP_P + (r // 4) + 1) + 4), yc_lo, ycT_ps)

            pe.wait_ge(gcol_ready, 2)
            with pe.Fori(0, OG // 2) as it:
                for j in range(2):
                    g = it * 2 + j
                    for k in range(KT):
                        if k == KT // 2:
                            pe.wait_ge(yc_lo, CT // 2)
                        k_tile((k + KT // 2) % KT, TILE_O + g * KT + k, k, GROUP_O + g, first=k == 0, last=k == KT - 1)
                        if j == 1 and k == GCOL_TILE:
                            gate_columns(it + 2, X[0], gate_sum)
                        if k == KT - 3:
                            pe.wait_ge(diag_ready, g + 1)
                            pe.wait_ge(gate_ready, ONE + 2 * g)
                            for ch in range(NCH):
                                m = nc.tensor.matmul(X[2 + ch][:], ones[:], gate_diag[:, 4 * ch:4 * ch + 4, :],
                                                     start=True, stop=True)
                            m.then_inc(gate_ps, 1)

        @block.scalar
        def _(act):
            def copy(dst, src):
                return nc.scalar.activation(dst, src, ACT.Copy)

            def high(count, slot, item_slot, kk, lands):
                act.wait_ge(raw_landed[item_slot], lands)
                act.wait_ge(hi_slot_free, count + 1)
                copy(whi[:, slot % HI], raw[:, item_slot, kk]).then_inc(hi_ready, 1)

            for s in (qkT_sb, w_ready, gate_ready):
                act.sem_inc(s, ONE)

            act.wait_ge(pool_step, 1)
            for n, v in enumerate((c[0], norm_g[0], b_ada[0, 0:D], b_ada[0, D:2 * D])):
                act.dma_start(param_rows[n * KT:(n + 1) * KT, :], v.rearrange("(k p) -> k p", p=P)).then_inc(params_landed, 16)
            for n, v in enumerate((ln_g[0], ln_b[0], b_dw[0])):
                act.dma_start(param_rows2[n * CT:(n + 1) * CT, :], v.rearrange("(k p) -> k p", p=P)).then_inc(params_landed, 16)
            act.dma_start(param_rows2[3 * CT:3 * CT + 1, :], q_norm_g).then_inc(params_landed, 16)
            act.dma_start(param_rows2[3 * CT + 1:3 * CT + 2, :], k_norm_g).then_inc(params_landed, 16)
            act.dma_start(param_rows2[3 * CT + 2:3 * CT + 2 + KT, :],
                          b_ada[0, 2 * D:3 * D].rearrange("(k p) -> k p", p=P)).then_inc(params_landed, 16)
            act.dma_start(tap_rows[0:TAPS, :], w_dw[0]).then_inc(taps_landed, 16)
            act.wait_ge(params_sb, 1)
            nc.scalar.activation(silu_c[:], cols[:, 0], ACT.Silu).then_inc(silu_ready, 1)
            act.wait_ge(ms_ready, 1)
            nc.scalar.activation(xstat[:, 6:8], xstat[:, 4:6], ACT.Sqrt).then_inc(rms_ready, 1)

            def x_scale(b):
                act.wait_ge(x_landed[b % 2], 16 * (b // 2 + 1))
                for t in range(TT):
                    nc.scalar.activation(x_block[:, b % 2, t], x_block[:, b % 2, t], ACT.Copy,
                                         scale=xstat[:, 8 + t:9 + t]).then_inc(x_scaled, 1)

            def x_high(b, q):
                act.wait_ge(h_ready, b * (BK // 2) + q + 1)
                copy(act_hi[:, b * BK + 2 * q:b * BK + 2 * q + 2], h32[:, q % 2]).then_inc(act_hi_ready, 1)

            def two_groups(b, kinds, it, body_items):
                k = 0
                for n, kind in enumerate(kinds):
                    if kind == "w":
                        for kk in range(2):
                            high(AG * BK * b + it * (GROUPS_PER_BODY * BK) + k, k, n % SLOTS, kk,
                                 landed(ITEM_A + b * BLOCK_ITEMS + n) + it * (body_items // SLOTS * 16))
                            k += 1

            act.wait_ge(rstd_ready, 1)
            x_scale(0)
            for q in range(BK // 2):
                x_high(0, q)
            for b in range(NB):
                body, end = (items_of(LAST_BODY), items_of(LAST_END)) if b == NB - 1 else (items_of(BODY), items_of(END))
                with act.Fori(0, BODIES) as it:
                    two_groups(b, body, it, len(body))
                if b < NB - 1:
                    x_scale(b + 1)
                two_groups(b, end, BODIES, len(body))
                if b < NB - 1:
                    for q in range(BK // 2):
                        x_high(b + 1, q)

            def pair_tile(g, k):
                high(TILE_B + g * KT + k, k, k // 2 % SLOTS, k % 2, landed_b(g, k // 2))

            def prepare_pair(step, g):
                if step == "squares":
                    act.wait_ge(bank_free, 4 * (GROUP_B + g + 1) + 4)
                    act.wait_ge(hstat_ready, ONE + g)
                    act.wait_ge(o_ps, ONE + 2 * g)
                    for t in range(TT):
                        for j in range(4):
                            i = nc.scalar.activation(squares[:, t * 4 + j], pair[:, t, j * HD:(j + 1) * HD], ACT.Square,
                                                     accum_out=hstat[:, 0, t * 4 + j:t * 4 + j + 1])
                            i.then_inc(sq_ready, 1)
                if step == "roots":
                    act.wait_ge(hstat_dve, 4 * g + 1)
                    nc.scalar.activation(hstat[:, 1], hstat[:, 0], ACT.Ln).then_inc(hstat_act, 1)
                    act.wait_ge(hstat_act, 2 * g + 1)
                    nc.scalar.activation(hstat[:, 1], hstat[:, 1], ACT.Exp, scale=-0.5).then_inc(hstat_act, 1)
                if step == "gate":
                    act.wait_ge(y_done, ONE + 2 * g)
                    nc.scalar.activation(sig[:], pair[:, :, 6 * HD:8 * HD], ACT.Silu).then_inc(sig_ready, 1)

            def attend(step, h, local):
                if step == "scale":
                    for t in range(TT):
                        for s in range(2):
                            j = 2 * s + local
                            seg = pair[:, t, j * HD:(j + 1) * HD]
                            i = nc.scalar.activation(seg, seg, ACT.Copy, scale=hstat[:, 2, t * 4 + j:t * 4 + j + 1])
                    i.then_inc(qk_scaled, 1)
                if step == "gains":
                    act.wait_ge(qkT_ps, h + 1)
                    act.wait_ge(z_ps, ONE + h)
                    nc.scalar.activation(qkT[:, 0], X[3][:, 0:T], ACT.Copy, scale=cols2[:, 3 * CT:3 * CT + 1])
                    nc.scalar.activation(qkT[:, 1], X[3][:, T:2 * T], ACT.Copy,
                                         scale=cols2[:, 3 * CT + 1:3 * CT + 2]).then_inc(qkT_sb, 1)
                if step == "soft":
                    act.wait_ge(z_ps, ONE + h + 1)
                    act.wait_ge(logw_ps, ONE + h)
                    nc.scalar.activation(absz, X[1][:, 0:3 * P], ACT.Abs).then_inc(abs_ready, 1)
                    act.wait_ge(abs_ready, h + 1)
                    nc.scalar.activation(absz[:], absz[:], ACT.Exp, scale=-1.0).then_inc(exp_ready, 1)
                    act.wait_ge(exp_ready, h + 1)
                    nc.scalar.activation(absz[:], absz[:], ACT.Ln, bias=1.0).then_inc(log_ready, 1)
                if step == "w":
                    act.wait_ge(logw_ps, ONE + h + 1)
                    act.wait_ge(o_ps, ONE + h)
                    nc.scalar.activation(wexp[:], X[1][:, 0:3 * P], ACT.Exp).then_inc(w_ready, 1)

            ACT_PREP = {4: "squares", 5: "roots", 6: "gate"}
            ACT_STEPS = {8: ("scale", 0), 12: ("gains", 0), 10: ("scale", 1), 15: ("soft", 0), 18: ("w", 0),
                         20: ("gains", 1), 24: ("soft", 1), 27: ("w", 1)}

            def glu_gates(n):
                if n < 4:
                    piece = glubuf[:, n // 2, n % 2]
                    nc.scalar.activation(piece, piece, ACT.Sigmoid).then_inc(gates_ready, 1)
                else:
                    piece = gatebuf[:, n // 2 - 2, n % 2]
                    nc.scalar.activation(piece, piece, ACT.Silu).then_inc(gates_ready, 1)

            for k in range(KT):
                pair_tile(0, k)
                if k == 0:
                    act.wait_ge(bank_free, 4 * GROUP_B + 4)
                if k < 8:
                    glu_gates(k)
                if 8 <= k < 8 + CT // 2:
                    r = k - 8
                    act.wait_ge(gluT_ps, r + 1)
                    copy(conv_in[:, 2 * r:2 * r + 2].rearrange("p c t -> p (c t)"), X[r % 2][:]).then_inc(gluT_sb, 1)
            with act.Fori(1, PAIRS) as g:
                for k in range(KT):
                    pair_tile(g, k)
                    if k in ACT_PREP:
                        prepare_pair(ACT_PREP[k], g - 1)
                    if k in ACT_STEPS:
                        step, local = ACT_STEPS[k]
                        if step == "scale":
                            act.wait_ge(hstat_ready, ONE + g)
                        attend(step, (g - 1) * 2 + local, local)

            last = 2 * (PAIRS - 1)
            for step in ("squares", "roots", "gate"):
                prepare_pair(step, PAIRS - 1)
            act.wait_ge(hstat_ready, ONE + PAIRS)
            attend("scale", last, 0)
            attend("scale", last + 1, 1)
            attend("gains", last, 0)
            attend("soft", last, 0)
            attend("w", last, 0)
            attend("gains", last + 1, 1)
            for n in range(4):
                act.wait_ge(xc_ready, n + 2)
                nc.scalar.activation(conv_in[:, 4 * n:4 * n + 4], conv_out[:, 4 * n:4 * n + 4], ACT.Square).then_inc(sqc_ready, 1)
            attend("soft", last + 1, 1)
            attend("w", last + 1, 1)
            act.wait_ge(var_ready, 1)
            nc.scalar.activation(ln_stat[:], ln_stat[:], ACT.Sqrt).then_inc(deviation_ready, 1)

            def swish(ct):
                if ct % 4 == 0:
                    act.wait_ge(norm_ready, ct // 4 + 1)
                nc.scalar.activation(conv_out[:, ct], conv_out[:, ct], ACT.Silu, scale=cols2[:, ct:ct + 1],
                                     bias=cols2[:, CT + ct:CT + ct + 1]).then_inc(swish_ready, 1)
                if ct % 2 == 1:
                    act.wait_ge(swish_ready, ct + 1)
                    copy(act_hi[:, ct - 1:ct + 1], conv_out[:, ct - 1:ct + 1]).then_inc(conv_hi, 1)

            for ct in range(CT):
                swish(ct)

            def y_high(r, ps, ready, tile, free=None):
                act.wait_ge(ps, r + 1)
                copy(act_hi[:, tile:tile + 2].rearrange("p c t -> p (c t)"), X[r % 2][:]).then_inc(ready, 1)

            weight_items = [n for n, kind in enumerate(P_ITEMS) if kind == "w"]
            for s in range(PG * PKT):
                n = weight_items[s // 2]
                high(TILE_P + s, s, n % SLOTS, s % 2, landed(ITEM_P + n) + EXTRA)
                if s >= 8 and s % 2 == 0 and s < 8 + CT:
                    r = (s - 8) // 2
                    y_high(r, ysbT_ps, ysb_hi, KT // 2 + 2 * r)
            act.wait_ge(bank_free, 4 * (GROUP_P + 2) + 4)
            for r in range(CT // 2):
                y_high(r, ycT_ps, yc_hi, 2 * r)
            weight_items = [n for n, kind in enumerate(O_BODY) if kind == "w"]
            with act.Fori(0, OG // 2) as it:
                for j in range(2):
                    g = it * 2 + j
                    for k in range(KT):
                        n = weight_items[j * (KT // 2) + k // 2]
                        high(TILE_O + g * KT + k, k, n % SLOTS, k % 2,
                             landed(ITEM_O + n) + EXTRA + it * (len(O_BODY) // SLOTS * 16))
                    act.wait_ge(gate_ps, ONE + g + 1)
                    act.wait_ge(bank_free, 4 * (GROUP_O + g) + 4)
                    for ch in range(NCH):
                        copy(gate_sb[:, ch * 512:(ch + 1) * 512], X[2 + ch][:]).then_inc(gate_ready, 1)

        @block.gpsimd
        def _(pool):
            nc.gpsimd.memset(param_rows2, 0.0).then_inc(pool_step, 1)
            for n, (dst, value) in enumerate(((ident, 0.0), (neg_tri, -1.0), (neg_ones, -1.0), (ones, 1.0), (never, 0.0), (ident_b, 0.0))):
                nc.gpsimd.memset(dst[:], value).then_inc(pool_step, 1)
            pool.wait_ge(pool_step, 7)
            nc.gpsimd.affine_select(out=ident[:], in_=ident[:], compare_op=ALU.not_equal, fill=1.0, base=0,
                                    pattern=[[-1, P]], channel_multiplier=1).then_inc(pool_step, 1)
            nc.gpsimd.affine_select(out=neg_tri[:], in_=neg_tri[:], compare_op=ALU.is_ge, fill=0.0, base=0,
                                    pattern=[[-1, P]], channel_multiplier=1).then_inc(pool_step, 1)
            nc.gpsimd.affine_select(out=never[:], in_=never[:], compare_op=ALU.is_gt, fill=NEVER, base=0,
                                    pattern=[[1, P]], channel_multiplier=-1).then_inc(pool_step, 1)
            nc.gpsimd.affine_select(out=ident_b[:], in_=ident_b[:], compare_op=ALU.not_equal, fill=1.0, base=0,
                                    pattern=[[-1, P]], channel_multiplier=1).then_inc(pool_step, 1)
            pool.wait_ge(pool_step, 11)
            nc.gpsimd.memset(wide[:], 0.0).then_inc(wide_zeroed, 1)
            pool.wait_ge(wide_zeroed, 1)
            pool.sem_inc(consts_ready, 1)
            for b in range(NB):
                pool.wait_ge(mod_summed, b + 1)
                nc.gpsimd.memset(wide[:], 0.0).then_inc(wide_zeroed, 1)

            pool.wait_ge(o_ps, ONE + 2 * PAIRS)
            pool.wait_ge(sig_ready, PAIRS)
            pool.wait_ge(y_done, ONE + 2 * PAIRS)
            pool.dma_start(wide[0:1, 0:CW], b_pw).then_inc(bpw_landed, 16)
            pool.wait_ge(var_ps, 1)
            nc.gpsimd.memset(gate_sum, 0.0).then_inc(gate_zeroed, 1)
            pool.wait_ge(gcol_ps, 2)
            nc.gpsimd.memset(gate_sum, 0.0).then_inc(gate_zeroed, 1)
            pool.wait_ge(conv_lo, CT // 2)
            for g in range(OG):
                pool.wait_ge(out_ready, g)
                pool.dma_start(x_res, x[0].rearrange("(t p) (g n) -> g p t n", p=P, n=GC)[g]).then_inc(xres_landed, 16)
                if g == 1:
                    pool.wait_ge(gcol_ps, 3)
                    nc.gpsimd.memset(gate_sum, 0.0).then_inc(gate_zeroed, 1)
                pool.wait_ge(out_ready, g + 1)
                pool.dma_start(out_rows[g], y_out).then_inc(stored, 16)
                pool.wait_ge(stored, 16 * (g + 1))
                pool.sem_inc(y_out_free, 1)

        @block.vector
        def _(dve):
            dve.sem_inc(bank_free, 4)
            for s in (y_done, hstat_ready):
                dve.sem_inc(s, ONE)
            dve.sem_inc(y_out_free, ONE)
            steps = [0]

            def then(instruction):
                steps[0] += 1
                instruction.then_inc(dve_step, 1)
                dve.wait_ge(dve_step, steps[0])

            def low(count, slot, item_slot, kk):
                dve.wait_ge(hi_ready, count + 1)
                dve.wait_ge(lo_slot_free, count + 1)
                nc.vector.tensor_tensor(wlo[:, slot % LO], raw[:, item_slot, kk],
                                        whi[:, slot % HI].bitcast(F32), ALU.subtract).then_inc(lo_ready, 1)

            dve.wait_ge(params_ps, 1)
            nc.vector.tensor_copy(cols[:].rearrange("p a k -> p (a k)"), X[0][:, 0:P])
            then(nc.vector.tensor_copy(cols2[:], X[0][:, P:P + 3 * CT + 2 + KT]))
            nc.vector.tensor_scalar(cols2[:, 3 * CT:3 * CT + 1], cols2[:, 3 * CT:3 * CT + 1], HD ** -0.5, None,
                                    ALU.mult).then_inc(params_sb, 1)
            dve.wait_ge(params_ps, 2)
            nc.vector.tensor_copy(taps[:].rearrange("p c k -> p (c k)"), X[1][:, 0:CT * TAPS]).then_inc(params_sb, 1)
            for n in range(4):
                dve.wait_ge(raw_landed[n], 16)
                piece = raw[:, n].rearrange("p a n -> p (a n)")
                nc.vector.tensor_tensor_reduce(out=piece, in0=piece, in1=piece, scale=1.0, scalar=0.0, op0=ALU.mult,
                                               op1=ALU.add, accum_out=xstat[:, n:n + 1]).then_inc(item_summed, 1)
            dve.wait_ge(item_summed, 4)
            halves = xstat[:, 0:4].rearrange("p (t h) -> p t h", h=2)
            then(nc.vector.tensor_tensor(xstat[:, 4:6], halves[:, :, 0], halves[:, :, 1], ALU.add))
            nc.vector.tensor_scalar(xstat[:, 4:6], xstat[:, 4:6], 1.0 / D, EPS, ALU.mult, ALU.add).then_inc(ms_ready, 1)
            dve.wait_ge(rms_ready, 1)
            nc.vector.reciprocal(xstat[:, 8:10], xstat[:, 6:8]).then_inc(rstd_ready, 1)
            dve.wait_ge(silu_ready, 1)
            dve.wait_ge(wide_zeroed, 1)

            def ada(k, item_slot, lands, summed):
                dve.wait_ge(raw_landed[item_slot], lands)
                dve.wait_ge(item_summed, summed)
                nc.vector.scalar_tensor_tensor(out=wide[:], in0=raw[:, item_slot].rearrange("p a n -> p (a n)"),
                                               scalar=k, in1=wide[:], op0=ALU.mult, op1=ALU.add).then_inc(item_summed, 1)

            for k in range(KT):
                n = ITEM_ADA0 + k
                ada(silu_c[:, k:k + 1], n % SLOTS, landed(n), n)

            def gate_item(sums, k, item_slot, lands, done):
                dve.wait_ge(raw_landed[item_slot], lands)
                dve.wait_ge(item_summed, SUM_LAST + done)
                nc.vector.scalar_tensor_tensor(out=sums, in0=raw[:, item_slot, 0], scalar=silu_c[:, bass.ds(k, 1)],
                                               in1=sums, op0=ALU.mult, op1=ALU.add).then_inc(gate_step, 1)
                dve.wait_ge(gate_step, done + 1)
                nc.vector.scalar_tensor_tensor(out=sums, in0=raw[:, item_slot, 1], scalar=silu_c[:, bass.ds(k + 1, 1)],
                                               in1=sums, op0=ALU.mult, op1=ALU.add).then_inc(item_summed, 1)

            def gate_column(n, ps):
                dve.wait_ge(gcol_ps, n + 1)
                bias = cols2[:, 3 * CT + 2:].rearrange("p (g j) -> p g j", g=OG)
                nc.vector.tensor_tensor(gate_cols[:, n], ps[:, 0:GC // P], bias[:, n], ALU.add).then_inc(gcol_ready, 1)

            def mod_columns(b):
                dve.wait_ge(mod_summed, b + 1)
                ks = slice(b * BK, (b + 1) * BK)
                nc.vector.tensor_tensor(mod_add[:], X[3][:, 0:BK], cols[:, 2, ks], ALU.add)
                then(nc.vector.tensor_tensor(mod_mul[:], X[3][:, BK:2 * BK], cols[:, 3, ks], ALU.add))
                then(nc.vector.scalar_tensor_tensor(out=mod_mul[:], in0=mod_mul[:], scalar=1.0, in1=cols[:, 1, ks],
                                                    op0=ALU.add, op1=ALU.mult))

            def affine(b, q):
                n = b * (BK // 2) + q
                dve.wait_ge(xT_ps, n + 1)
                if n >= 2:
                    dve.wait_ge(act_hi_ready, n - 1)
                    dve.wait_ge(act_lo_ready, n - 1)
                for kk in range(2):
                    k = 2 * q + kk
                    i = nc.vector.tensor_scalar(h32[:, q % 2, kk], X[q % 3][:, kk * T:(kk + 1) * T],
                                                mod_mul[:, k:k + 1], mod_add[:, k:k + 1], ALU.mult, ALU.add)
                i.then_inc(h_ready, 1)

            def x_low(b, q):
                dve.wait_ge(act_hi_ready, b * (BK // 2) + q + 1)
                dve.wait_ge(h_ready, b * (BK // 2) + q + 1)
                ks = slice(b * BK + 2 * q, b * BK + 2 * q + 2)
                nc.vector.tensor_tensor(act_lo[:, ks], h32[:, q % 2], act_hi[:, ks].bitcast(F32),
                                        ALU.subtract).then_inc(act_lo_ready, 1)

            def two_groups(b, kinds, it, after):
                body_items = len(items_of(LAST_BODY if b == NB - 1 else BODY))
                n = k = a_items = 0
                for kind in kinds:
                    group = AG * b + it * GROUPS_PER_BODY + (k - 1) // BK
                    lands = landed(ITEM_A + b * BLOCK_ITEMS + n) + it * (body_items // SLOTS * 16)
                    if kind == "w":
                        for kk in range(2):
                            low(AG * BK * b + it * (GROUPS_PER_BODY * BK) + k, k, n % SLOTS, kk)
                            for step, *which in after.get(k, ()):
                                step(b + 1, *which)
                            k += 1
                        n += 1
                    elif kind == "a" and b == NB - 1:
                        done = it * LAST_BODY.count("a") + a_items
                        gate_item(gate_sum0, done * 2, n % SLOTS, lands, done)
                        a_items += 1
                        n += 1
                    elif kind == "a":
                        kt = it * A_PER_BODY + a_items
                        ada(silu_c[:, bass.ds(kt, 1)], n % SLOTS, lands, SUM_A + KT * b + kt)
                        a_items += 1
                        n += 1
                    else:
                        for t in range(TT):
                            if t == 0:
                                dve.wait_ge(half_done, group + 1)
                            else:
                                dve.wait_ge(lo_slot_free, AG * BK * b + it * (GROUPS_PER_BODY * BK) + k + LO)
                            for ch in range(NCH):
                                dst = cbuf[:, it * GROUPS_PER_BODY + (k - 1) // BK, t, ch * 512:(ch + 1) * 512]
                                if b == 0:
                                    nc.vector.tensor_copy(dst, U[:, t * NCH + ch]).then_inc(bank_free, 1)
                                else:
                                    nc.vector.tensor_tensor(dst, dst, U[:, t * NCH + ch], ALU.add).then_inc(bank_free, 1)

            mod_columns(0)
            for q in range(BK // 2):
                affine(0, q)
                if q:
                    x_low(0, q - 1)
            x_low(0, BK // 2 - 1)
            for b in range(NB):
                dve.wait_ge(wide_zeroed, b + 2)
                with dve.Fori(0, BODIES) as it:
                    two_groups(b, LAST_BODY if b == NB - 1 else BODY, it, {})
                two_groups(b, LAST_END if b == NB - 1 else END, BODIES, {} if b == NB - 1 else {
                    13: [(mod_columns,), (affine, 0), (affine, 1)],
                    14: [(x_low, 0), (affine, 2)],
                    15: [(x_low, 1), (affine, 3), (x_low, 2), (x_low, 3)]})

            def empty_group(group, tiles, place):
                for t in range(TT):
                    if t == 0:
                        dve.wait_ge(half_done, group + 1)
                    else:
                        dve.wait_ge(lo_slot_free, tiles + LO)
                    for ch in range(NCH):
                        place(U[:, t * NCH + ch], t, slice(ch * 512, (ch + 1) * 512)).then_inc(bank_free, 1)

            def conv_tap(g, n):
                a, shift = n % 2, n // 2
                ct = 2 * g + a
                weight = taps[:, ct, TAPS - 1 - shift:TAPS - shift]
                if shift == 0:
                    nc.vector.tensor_scalar(conv_out[:, ct, :], conv_in[:, ct, :], weight, b_dw_col(g, a),
                                            ALU.mult, ALU.add).then_inc(conv_step, 1)
                else:
                    dve.wait_ge(conv_step, 2 * TAPS * g + n - 1)
                    nc.vector.scalar_tensor_tensor(out=conv_out[:, ct, shift:T], in0=conv_in[:, ct, 0:T - shift],
                                                   scalar=weight, in1=conv_out[:, ct, shift:T],
                                                   op0=ALU.mult, op1=ALU.add).then_inc(conv_step, 1)

            def b_dw_col(g, a):
                return cols2[:, bass.ds(2 * CT + 2 * g + a, 1)]

            def prepare_pair(step, p):
                if step == "mean":
                    dve.wait_ge(sq_ready, 8 * (p + 1))
                    nc.vector.tensor_scalar(hstat[:, 0], hstat[:, 0], 1.0 / HD, EPS, ALU.mult, ALU.add).then_inc(hstat_dve, 1)
                if step == "newton":
                    dve.wait_ge(hstat_act, 2 * (p + 1))
                    nc.vector.tensor_tensor(hstat[:, 2], hstat[:, 1], hstat[:, 1], ALU.mult).then_inc(hstat_dve, 1)
                    dve.wait_ge(hstat_dve, 4 * p + 2)
                    nc.vector.tensor_tensor(hstat[:, 2], hstat[:, 2], hstat[:, 0], ALU.mult).then_inc(hstat_dve, 1)
                    dve.wait_ge(hstat_dve, 4 * p + 3)
                    nc.vector.tensor_scalar(hstat[:, 2], hstat[:, 2], -0.5, 1.5, ALU.mult, ALU.add).then_inc(hstat_dve, 1)
                    dve.wait_ge(hstat_dve, 4 * p + 4)
                    nc.vector.tensor_tensor(hstat[:, 2], hstat[:, 2], hstat[:, 1], ALU.mult).then_inc(hstat_ready, 1)

            def attend(step, p, local):
                h = 2 * p + local
                if step == "soft":
                    dve.wait_ge(log_ready, h + 1)
                    nc.vector.scalar_tensor_tensor(out=absz, in0=X[1][:, 0:3 * P], scalar=0.0, in1=absz,
                                                   op0=ALU.max, op1=ALU.add).then_inc(soft_ready, 1)
                if step == "y":
                    dve.wait_ge(o_ps, ONE + h + 1)
                    dve.wait_ge(sig_ready, p + 1)
                    nc.vector.tensor_tensor(ysb[:, :, bass.ds(h * HD, HD)], X[2][:, 0:T].rearrange("p (t d) -> p t d", t=TT),
                                            sig[:, :, local * HD:(local + 1) * HD], ALU.mult).then_inc(y_done, 1)

            DVE_PREP = {3: "mean", 4: "newton"}
            DVE_STEPS = {14: ("soft", 0), 19: ("y", 0), 23: ("soft", 1), 28: ("y", 1)}
            CONV_STEPS = 2 * TAPS

            def keep_pair(bank, t, columns):
                return nc.vector.tensor_copy(pair[:, t, columns], bank)

            def split_pair_tile(g, k):
                low(TILE_B + g * KT + k, k, k // 2 % SLOTS, k % 2)

            for k in range(KT):
                split_pair_tile(0, k)
                if k == 0:
                    dve.wait_ge(bank_free, 4 * GROUP_B + 4)
                if k == 8:
                    gate_column(0, X[3])
                if 1 <= k <= 4:
                    n = k - 1
                    dve.wait_ge(gates_ready, n + 1)
                    u, gate = ubuf[:, n // 2, n % 2], glubuf[:, n // 2, n % 2]
                    nc.vector.tensor_tensor(u, u, gate, ALU.mult).then_inc(glu_ready, 1)
                if k >= KT // 2:
                    if k == KT // 2:
                        dve.wait_ge(gluT_sb, CT // 2)
                    for n in range(4 * (k - KT // 2), min(4 * (k - KT // 2) + 4, CONV_STEPS)):
                        conv_tap(0, n)
            empty_group(GROUP_B, TILE_B + KT, keep_pair)
            with dve.Fori(1, PAIRS) as g:
                n = 0
                for k in range(KT):
                    split_pair_tile(g, k)
                    if k in DVE_PREP:
                        prepare_pair(DVE_PREP[k], g - 1)
                    if k in DVE_STEPS:
                        attend(DVE_STEPS[k][0], g - 1, DVE_STEPS[k][1])
                    for _ in range(2 if k else 0):
                        conv_tap(g, n)
                        n += 1
                empty_group(GROUP_B + g, TILE_B + g * KT + KT, keep_pair)

            p = PAIRS - 1
            for step in ("mean", "newton"):
                prepare_pair(step, p)
            dve.wait_ge(mean_ps, 1)
            nc.vector.tensor_scalar(ln_stat[:], X[0][:, 0:T], 1.0 / CW, None, ALU.mult).then_inc(xc_ready, 1)
            attend("soft", p, 0)
            dve.wait_ge(xc_ready, 1)
            across = ln_stat[:].unsqueeze(1).to_broadcast([P, 4, T])
            for n in range(4):
                part = conv_out[:, 4 * n:4 * n + 4]
                nc.vector.tensor_tensor(part, part, across, ALU.add).then_inc(xc_ready, 1)
            attend("y", p, 0)
            attend("soft", p, 1)
            dve.wait_ge(var_ps, 1)
            nc.vector.tensor_scalar(ln_stat[:], X[0][:, 0:T], 1.0 / CW, EPS, ALU.mult, ALU.add).then_inc(var_ready, 1)
            attend("y", p, 1)
            dve.wait_ge(deviation_ready, 1)
            then(nc.vector.reciprocal(ln_stat[:], ln_stat[:]))
            dve.wait_ge(sqc_ready, 4)
            for n in range(4):
                part = conv_out[:, 4 * n:4 * n + 4]
                nc.vector.tensor_tensor(part, part, across, ALU.mult).then_inc(norm_ready, 1)
            for r in range(CT // 2):
                dve.wait_ge(conv_hi, r + 1)
                two = slice(2 * r, 2 * r + 2)
                nc.vector.tensor_tensor(act_lo[:, two], conv_out[:, two], act_hi[:, two].bitcast(F32),
                                        ALU.subtract).then_inc(conv_lo, 1)
                if r == 0:
                    dve.wait_ge(gate_zeroed, 1)
                if r < TAIL_ITEMS:
                    gate_item(gate_sum, 2 * r, r % SLOTS, landed(ITEM_P + r) + EXTRA, GATE_ITEMS + r)

            def y_low(r, high_ready, ready, tile):
                dve.wait_ge(high_ready, r + 1)
                two = slice(tile, tile + 2)
                nc.vector.tensor_tensor(act_lo[:, two].rearrange("p c t -> p (c t)"), X[r % 2][:],
                                        act_hi[:, two].bitcast(F32).rearrange("p c t -> p (c t)"),
                                        ALU.subtract).then_inc(ready, 1)

            s, gates_done = 0, TAIL_ITEMS
            for n, kind in enumerate(P_ITEMS):
                if kind == "a":
                    if n >= TAIL_ITEMS:
                        gate_item(gate_sum, 2 * gates_done, n % SLOTS, landed(ITEM_P + n) + EXTRA, GATE_ITEMS + gates_done)
                        gates_done += 1
                    continue
                for kk in range(2):
                    low(TILE_P + s, s, n % SLOTS, kk)
                    if s >= 7 and s % 2 == 1 and s < 7 + CT:
                        r = (s - 7) // 2
                        y_low(r, ysb_hi, ysb_lo, KT // 2 + 2 * r)
                    if s == PG * PKT - 1:
                        gate_column(1, X[3])
                    if s % PKT == PKT - 1:
                        gates = gatebuf[:, s // PKT]
                        empty_group(GROUP_P + s // PKT, TILE_P + s + 1, lambda bank, t, columns: nc.vector.tensor_tensor(
                            gates[:, t, columns], gates[:, t, columns], bank, ALU.mult))
                    s += 1
            for r in range(CT // 2):
                y_low(r, yc_hi, yc_lo, 2 * r)

            with dve.Fori(0, OG // 2) as it:
                dve.wait_ge(gate_zeroed, it + 2)
                k = a_items = 0
                for n, kind in enumerate(O_BODY):
                    lands = landed(ITEM_O + n) + EXTRA + it * (len(O_BODY) // SLOTS * 16)
                    if kind == "a":
                        gate_item(gate_sum, 2 * a_items, n % SLOTS, lands, 2 * GATE_ITEMS + it * GATE_ITEMS + a_items)
                        a_items += 1
                        continue
                    for kk in range(2):
                        g = it * 2 + k // KT
                        low(TILE_O + it * (2 * KT) + k, k, n % SLOTS, kk)
                        if k == KT + GCOL_TILE + 2:
                            gate_column(it + 2, X[0])
                        if k % KT == KT - 4:
                            dve.wait_ge(gate_ps, ONE + g)
                            dve.wait_ge(gcol_ready, it + 3 if k > KT else it + 2)
                            nc.vector.tensor_tensor(gate_diag, ident[:].unsqueeze(1).to_broadcast([P, GC // P, P]),
                                                    gate_cols[:, g].unsqueeze(2).to_broadcast([P, GC // P, P]),
                                                    ALU.mult).then_inc(diag_ready, 1)
                        if k % KT == KT - 1:
                            dve.wait_ge(gate_ready, ONE + 2 * g + 2)
                            dve.wait_ge(y_out_free, ONE + g)
                            empty_group(GROUP_O + g, TILE_O + it * (2 * KT) + k + 1, lambda bank, t, columns: nc.vector.tensor_tensor(
                                y_out[:, t, columns], bank, gate_sb[:, columns], ALU.mult))
                            dve.wait_ge(xres_landed, 16 * g + 16)
                            dve.wait_ge(bank_free, 4 * (GROUP_O + g + 1) + 4)
                            nc.vector.tensor_tensor(y_out, y_out, x_res, ALU.add).then_inc(out_ready, 1)
                        k += 1


_INS = ["x", "c", "norm_g", "w_ada", "b_ada", "w_in", "q_norm_g", "k_norm_g", "w_dw", "b_dw", "ln_g", "ln_b",
        "w_pw", "b_pw", "w_out"]


def kernel(**inputs):
    import concourse.bacc as bacc
    from concourse.bass_utils import run_bass_kernel_spmd

    nc = bacc.Bacc("TRN2", target_bir_lowering=False, num_devices=1)
    arrays, args = {}, []
    for name in _INS:
        a = np.ascontiguousarray(inputs[name])
        arrays[f"in_{name}"] = a
        args.append(nc.dram_tensor(f"in_{name}", a.shape, mybir.dt.from_np(a.dtype), kind="ExternalInput").ap())
    out = nc.dram_tensor("out_x", (1, T, D), F32, kind="ExternalOutput").ap()
    hybrid_layer(nc, *args, out)
    r = run_bass_kernel_spmd(nc, [arrays], core_ids=[0])
    return r.results[0]["out_x"]
```

```python
import numpy as np
from contextlib import ExitStack

import concourse.bass as bass
from concourse import mybir

F32 = mybir.dt.float32
BF16 = mybir.dt.bfloat16
F32R = mybir.dt.float32r
ACT = mybir.ActivationFunctionType
ALU = mybir.AluOpType

P = 128
D = 4096
T = 256
TT = T // P
HD = 128
SBW = D // 2
CW = D - SBW
TAPS = 31
EPS = 1e-6
NEVER = -2.0 ** 100
ONE = 1
KT = D // P
GC = 1024
NCH = GC // 512
BK = 8
NB = KT // BK
AG = 3 * CW // GC
PAIRS = SBW // (2 * HD)
PG = CW // GC
PKT = CW // P
OG = D // GC
CT = CW // P
SLOTS = 4
HI = 4
LO = 2

BODY = ("w", "a", "w", "a", "a", "w", "a", "a", "w", "a", "e") * 2
END = ("w", "a", "w", "a", "a", "w", "a", "w", "a", "e", "w", "a", "w", "a", "a", "w", "w", "e")
LAST_BODY = ("w", "a", "w", "a", "w", "w", "e", "w", "a", "w", "w", "a", "w", "e")
LAST_END = ("w", "a", "w", "a", "w", "a", "w", "a", "e", "w", "a", "w", "a", "w", "a", "w", "a", "e")
PAIR_BODY = ("w", "a", "w") * 2 + ("w", "a") * 4 + ("w", "a", "w") * 2 + ("w",) * 4
P_ITEMS = ("w", "a", "w") * 8
O_BODY = ("w", "a", "w") * 7 + ("a", "w", "w")
O_LAST = ("w",) * (KT // 2)
GATE_ITEMS = 16
GROUPS_PER_BODY = 2
BODIES = AG // GROUPS_PER_BODY - 1

ITEM_A = KT
BODY_ITEMS = BODY.count("w") + BODY.count("a")
A_PER_BODY = BODY.count("a")
BLOCK_ITEMS = BODIES * BODY_ITEMS + END.count("w") + END.count("a")
LAST_ITEMS = BODIES * (LAST_BODY.count("w") + LAST_BODY.count("a")) + LAST_END.count("w") + LAST_END.count("a")
ITEM_B = ITEM_A + (NB - 1) * BLOCK_ITEMS + LAST_ITEMS
B_ITEMS = PAIRS * KT // 2 + 2 * PAIR_BODY.count("a")
ITEM_P = ITEM_B + B_ITEMS
ITEM_O = ITEM_P + len(P_ITEMS)
SUM_A = KT
SUM_LAST = NB * KT
SUM_B = SUM_LAST + GATE_ITEMS
SUM_P = SUM_B + GATE_ITEMS
SUM_O = SUM_P + GATE_ITEMS // 2
TILE_B = AG * KT
TILE_P = TILE_B + PAIRS * KT
TILE_O = TILE_P + PG * PKT
GROUP_B = AG * NB
GROUP_P = GROUP_B + PAIRS
GROUP_O = GROUP_P + PG
SB_ROUNDS = [3 + 3 * r for r in range(CT // 2 - 1)]
LATE_ROUNDS = [1 + 2 * n for n in range(CT // 2 + 1)]
ITEM_O1 = ITEM_O + len(O_BODY)
ITEM_O3 = ITEM_O1 + (OG - 2) * len(O_BODY)
SUM_O1 = SUM_O + GATE_ITEMS // 2
CONV_FIRST, CONV_LOOP1, CONV_LOOP2 = 2, 3, 1
LOOP1_END = PAIRS - 3
PAIR_ITEMS = ("w",) * (KT // 2)




def held(tail, kinds, n):
    history = tail + kinds
    return history[n], history[SLOTS:n + 1].count(history[n]) if n >= SLOTS else -history[n + 1:SLOTS].count(history[n])


def items_of(body):
    return [kind for kind in body if kind != "e"]


def hybrid_layer(nc, x, c, norm_g, w_ada, b_ada, w_in, q_norm_g, k_norm_g,
                 w_dw, b_dw, ln_g, ln_b, w_pw, b_pw, w_out, out):
    x_rows = x[0].rearrange("(t p) n -> p t n", p=P)
    out_rows = out[0].rearrange("(t p) (g n) -> g p t n", p=P, n=GC)
    ada_rows = w_ada[0].rearrange("(k p) (s b n) -> k p s b n", p=P, s=3, b=NB)
    gate_pairs = w_ada[0][:, 2 * D:3 * D].rearrange("(k two p) (g n) -> k p g two n", p=P, two=2, n=GC)
    conv_rows = w_in[0][:, 4 * SBW:].rearrange("(k p) (g n) -> g p k n", p=P, n=GC)
    pair_rows = w_in[0][:, 0:4 * SBW].rearrange("(k p) (r g n) -> g k p r n", p=P, r=4, n=2 * HD)
    pw_rows = w_pw[0].rearrange("(k p) (g n) -> g p k n", p=P, n=GC)
    wo_rows = w_out[0].rearrange("(k p) (g n) -> g p k n", p=P, n=GC)

    ctx = ExitStack()
    with ctx:
        def sb(name, shape, dt=F32):
            return ctx.enter_context(nc.sbuf_tensor(name, shape, dt))

        def bank(name, shape):
            return ctx.enter_context(nc.psum_tensor(name, shape, F32))

        def sem(name):
            return ctx.enter_context(nc.semaphore(name))

        act_hi = sb("act_hi", [P, KT, T], F32R)
        act_lo = sb("act_lo", [P, KT, T], F32R)
        raw = sb("raw", [P, SLOTS, 2, GC])
        whi = sb("whi", [P, HI, GC], F32R)
        wlo = sb("wlo", [P, LO, GC], F32R)
        cbuf = sb("cbuf", [P, AG, TT, GC])
        wide = sb("wide", [P, 2 * GC])
        ysb = sb("ysb", [P, TT, SBW])
        tmp = sb("tmp", [P, 2, 2, T])
        wexp = sb("wexp", [P, 3 * P])
        ident = sb("ident", [P, P])
        neg_tri = sb("neg_tri", [P, P])
        neg_ones = sb("neg_ones", [P, P])
        ones = sb("ones", [P, P])
        never = sb("never", [P, P], BF16)
        ident_b = sb("ident_b", [P, P], BF16)
        cols = sb("cols", [P, 4, KT])
        cols2 = sb("cols2", [P, 3 * CT + 2 + KT])
        gate_cols = sb("gate_cols", [P, OG, GC // P])
        taps = sb("taps", [P, CT, TAPS])
        silu_c = sb("silu_c", [P, KT])
        xstat = sb("xstat", [P, TT, NB + 4])
        mod_mul = sb("mod_mul", [P, BK])
        mod_add = sb("mod_add", [P, BK])
        hstat = sb("hstat", [P, 3, 8])
        sig = sb("sig", [P, TT, 2 * HD])
        ln_stat = sb("ln_stat", [P, T])
        ubuf, glubuf, gatebuf = cbuf[:, 0:2], cbuf[:, 2:4], cbuf[:, 4:6]

        x_block = [cbuf[:, AG - 2], cbuf[:, AG - 1]] + [ysb[:, b].rearrange("p (t n) -> p t n", t=TT) for b in range(2)]
        x_sums, x_pair_sums = xstat[:, :, 0:NB], xstat[:, :, NB:NB + 2]
        x_ms, x_rms, x_rstd = xstat[:, :, NB + 2], xstat[:, :, NB + 3], xstat[:, :, NB]
        h32 = tmp
        qkT = tmp[:, 0]
        absz = tmp[:, 1].rearrange("p a t -> p (a t)")[:, 0:3 * P]
        pair = wide[:].rearrange("p (t n) -> p t n", t=TT)
        conv_in = glubuf.rearrange("p a t n -> p (a t n)").rearrange("p (c t) -> p c t", t=T)
        conv_out = ubuf.rearrange("p a t n -> p (a t n)").rearrange("p (c t) -> p c t", t=T)
        squares = tmp[:].rearrange("p a b (c n) -> p (a b c) n", n=P)
        gate_sum0 = wide[:, 0:GC]
        gate_sum1 = ysb[:, :, SBW - 4 * HD:]
        gate_sum = cbuf[:, 3, 0]
        gate_diag = cbuf[:, 3, 1].rearrange("p (j n) -> p j n", n=P)
        gate_sb = tmp[:].rearrange("p a b t -> p (a b t)")
        x_res = cbuf[:, 0]
        y_out = cbuf[:, 2]
        bias_row = cbuf[0:1, 2].rearrange("p t n -> p (t n)")
        param_rows = raw[:, SLOTS - 1, 0, 0:P]
        param_rows2 = raw[:, SLOTS - 1, 0, P:2 * P]
        tap_rows = cbuf[:, 2].rearrange("p t n -> p (t n)")

        U = bank("U", [P, 4, 512])
        X = [bank(f"X{i}", [P, 512]) for i in range(4)]

        raw_landed = [sem(f"raw_landed{i}") for i in range(SLOTS)]
        params_landed, taps_landed = sem("params_landed"), sem("taps_landed")
        x_landed = [sem(f"x_landed{b}") for b in range(NB)]
        x_squared = sem("x_squared")
        xres_landed = sem("xres_landed")
        bpw_landed, stored = sem("bpw_landed"), sem("stored")
        item_summed = sem("item_summed")
        hi_ready, lo_ready = sem("hi_ready"), sem("lo_ready")
        hi_slot_free, lo_slot_free = sem("hi_slot_free"), sem("lo_slot_free")
        bank_free, half_done = sem("bank_free"), sem("half_done")
        consts_ready, pool_step = sem("consts_ready"), sem("pool_step")
        params_ps, params_sb, silu_ready = sem("params_ps"), sem("params_sb"), sem("silu_ready")
        ms_ready, rms_ready, rstd_ready = sem("ms_ready"), sem("rms_ready"), sem("rstd_ready")
        dve_step = sem("dve_step")
        mod_summed, wide_zeroed, mod_ready = sem("mod_summed"), sem("wide_zeroed"), sem("mod_ready")
        x_scaled, xT_ps, h_ready = sem("x_scaled"), sem("xT_ps"), sem("h_ready")
        act_hi_ready, act_lo_ready = sem("act_hi_ready"), sem("act_lo_ready")
        gates_ready, glu_ready, gluT_ps, gluT_sb = sem("gates_ready"), sem("glu_ready"), sem("gluT_ps"), sem("gluT_sb")
        conv_step = sem("conv_step")
        sq_ready, hstat_act, hstat_dve, hstat_ready = sem("sq_ready"), sem("hstat_act"), sem("hstat_dve"), sem("hstat_ready")
        sig_ready, qk_scaled = sem("sig_ready"), sem("qk_scaled")
        qkT_ps, qkT_sb, z_ps, abs_ready = sem("qkT_ps"), sem("qkT_sb"), sem("z_ps"), sem("abs_ready")
        exp_ready, log_ready, soft_step, soft_ready = sem("exp_ready"), sem("log_ready"), sem("soft_step"), sem("soft_ready")
        logw_ps, w_ready, o_ps, y_done = sem("logw_ps"), sem("w_ready"), sem("o_ps"), sem("y_done")
        mean_ps, xc_ready, sqc_ready, var_ps = sem("mean_ps"), sem("xc_ready"), sem("sqc_ready"), sem("var_ps")
        var_ready, deviation_ready = sem("var_ready"), sem("deviation_ready")
        norm_ready, swish_ready = sem("norm_ready"), sem("swish_ready")
        conv_hi, conv_lo = sem("conv_hi"), sem("conv_lo")
        ysbT_ps, ysb_hi, ysb_lo = sem("ysbT_ps"), sem("ysb_hi"), sem("ysb_lo")
        ycT_ps, yc_hi, yc_lo = sem("ycT_ps"), sem("yc_hi"), sem("yc_lo")
        gate_step, gate_zeroed, gcol_ps, gcol_ready = sem("gate_step"), sem("gate_zeroed"), sem("gcol_ps"), sem("gcol_ready")
        diag_ready, gate_ps, gate_ready = sem("diag_ready"), sem("gate_ps"), sem("gate_ready")
        out_ready, y_out_free = sem("out_ready"), sem("y_out_free")

        block = ctx.enter_context(nc.Block())

        @block.sync
        def _(sp):
            def reserve(summed=None, split=None):
                if summed is not None:
                    sp.wait_ge(item_summed, summed)
                if split is not None:
                    if not isinstance(split, int):
                        split = sp.snap(split)
                        sp.wait_ge(params_ps, 1)
                    sp.wait_ge(lo_ready, split)

            def load(slot, dst, src, **used):
                reserve(**used)
                sp.dma_start(dst, src).then_inc(raw_landed[slot], 16)

            for b in range(NB):
                if b == 1:
                    sp.wait_ge(taps_landed, 16)
                    sp.wait_ge(params_landed, 16 * 10)
                sp.dma_start(x_block[b], x_rows[:, :, b * BK * P:(b + 1) * BK * P]).then_inc(x_landed[b], 16)
            for k in range(KT):
                if k == SLOTS - 1:
                    sp.wait_ge(params_ps, 1)
                load(k % SLOTS, raw[:, k % SLOTS], ada_rows[k, :, 0:2, 0, :], summed=k - SLOTS + 1 if k >= SLOTS else None)

            def wait_of(tail, kinds, n, tiles, sums):
                kind, number = held(tail, kinds, n)
                return dict(summed=sums + number) if kind == "a" else dict(split=tiles + 2 * number)

            tail = ["a"] * SLOTS
            for b in range(NB):
                body, end = (items_of(LAST_BODY), items_of(LAST_END)) if b == NB - 1 else (items_of(BODY), items_of(END))
                sums = SUM_A + KT * b

                def load_item(n, it):
                    wait = wait_of(tail, body + end, n, BK * AG * b + it * (BK * GROUPS_PER_BODY),
                                   sums + it * body.count("a"))
                    kinds = body + end
                    w, a, slot = kinds[:n].count("w"), kinds[:n].count("a") + it * body.count("a"), n % SLOTS
                    if kinds[n] == "w":
                        g, k0 = w // (BK // 2), b * BK + 2 * (w % (BK // 2))
                        load(slot, raw[:, slot], conv_rows[it * GROUPS_PER_BODY + g, :, k0:k0 + 2, :], **wait)
                    elif b < NB - 1:
                        load(slot, raw[:, slot], ada_rows[a, :, 0:2, b + 1, :], **wait)
                    else:
                        load(slot, raw[:, slot], gate_pairs[a, :, 0], **wait)

                for n in range(SLOTS):
                    load_item(n, 0)
                with sp.Fori(0, BODIES) as it:
                    for n in range(SLOTS, len(body) + SLOTS):
                        load_item(n, it)
                for n in range(len(body) + SLOTS, len(body) + len(end)):
                    load_item(n, BODIES - 1)
                tail = end[-SLOTS:]

            def load_pair(g, kinds, tail, sums, gates=None):
                for n, kind in enumerate(kinds):
                    before = kinds[:n].count(kind)
                    reserve(**wait_of(list(tail), list(kinds), n, TILE_B + g * KT, sums))
                    for kk in range(2):
                        dst = raw[:, n % SLOTS, kk]
                        if kind == "w":
                            sp.dma_start(dst.rearrange("p (r n) -> p r n", r=4),
                                         pair_rows[g, 2 * before + kk]).then_inc(raw_landed[n % SLOTS], 16)
                        else:
                            sp.dma_start(dst, gate_pairs[gates(before), :, 1, kk]).then_inc(raw_landed[n % SLOTS], 16)

            ALL_WEIGHTS = ("w",) * SLOTS
            load_pair(0, PAIR_ITEMS, tail, SUM_B)
            with sp.Fori(1, LOOP1_END) as g:
                load_pair(g, PAIR_ITEMS, ALL_WEIGHTS, SUM_B)
            with sp.Fori(LOOP1_END, PAIRS - 1) as g:
                before = (g - LOOP1_END) * (GATE_ITEMS // 2)
                load_pair(g, PAIR_BODY, ALL_WEIGHTS, SUM_B + before, lambda n: before + n)
            load_pair(PAIRS - 1, PAIR_ITEMS, ALL_WEIGHTS, SUM_P)

            def load_list(kinds, tail, tiles, sums, weights, gates):
                for n, kind in enumerate(kinds):
                    before = kinds[:n].count(kind)
                    load(n % SLOTS, raw[:, n % SLOTS], weights(before) if kind == "w" else gates(before),
                         **wait_of(list(tail), list(kinds), n, tiles, sums))

            load_list(P_ITEMS, ALL_WEIGHTS, TILE_P, SUM_P,
                      lambda n: pw_rows[n // (PKT // 2), :, 2 * (n % (PKT // 2)):2 * (n % (PKT // 2)) + 2, :],
                      lambda n: gate_pairs[n, :, 2])
            load_list(O_BODY, P_ITEMS[-SLOTS:], TILE_O, SUM_O, lambda n: wo_rows[0, :, 2 * n:2 * n + 2, :],
                      lambda n: gate_pairs[GATE_ITEMS // 2 + n, :, 2])
            with sp.Fori(1, OG - 1) as g:
                load_list(O_BODY, O_BODY[-SLOTS:], TILE_O + g * KT, SUM_O1 + (g - 1) * (GATE_ITEMS // 2),
                          lambda n: wo_rows[g, :, 2 * n:2 * n + 2, :],
                          lambda n: gate_pairs[(g - 1) * (GATE_ITEMS // 2) + n, :, 3])
            load_list(O_LAST, O_BODY[-SLOTS:], TILE_O + (OG - 1) * KT, SUM_O1 + GATE_ITEMS,
                      lambda n: wo_rows[OG - 1, :, 2 * n:2 * n + 2, :], None)

        def landed(item):
            return 16 * (item // SLOTS + 1)

        def landed_b(before, n):
            return 16 * (ITEM_B // SLOTS) + 32 * (before // SLOTS + n // SLOTS + 1)

        def landed_first(g, n):
            return landed_b(0, n)

        def landed_loop1(g, n):
            return landed_b(0, n) + g * (len(PAIR_ITEMS) // SLOTS * 32)

        def landed_loop2(g, n):
            return landed_b(LOOP1_END * len(PAIR_ITEMS), n) + (g - LOOP1_END) * (len(PAIR_BODY) // SLOTS * 32)

        def landed_last(g, n):
            return landed_b(B_ITEMS - len(PAIR_ITEMS), n)

        EXTRA = 16 * (B_ITEMS // SLOTS)

        @block.tensor
        def _(pe):
            pe.sem_inc(hi_slot_free, HI)
            pe.sem_inc(lo_slot_free, LO)
            for s in (z_ps, logw_ps, o_ps, gate_ps):
                pe.sem_inc(s, ONE)

            def k_tile(tile, count, slot, group=None, first=False, last=False, seeded=False):
                hi, lo = whi[:, slot % HI], wlo[:, slot % LO]
                pe.wait_ge(hi_ready, count + 1)
                if last:
                    pe.wait_ge(lo_ready, count + 1)
                    for t in range(TT):
                        for part, weights in ((act_hi, hi), (act_lo, hi), (act_hi, lo)):
                            for ch in range(NCH):
                                m = nc.tensor.matmul(U[:, t * NCH + ch], part[:, tile, t * P:(t + 1) * P],
                                                     weights[:, ch * 512:(ch + 1) * 512],
                                                     start=False, stop=weights is lo)
                                if t == TT - 1 and weights is lo and ch == 0:
                                    m.then_inc(hi_slot_free, 1)
                        m.then_inc(lo_slot_free if t == TT - 1 else half_done, 1)
                    return
                for t in range(TT):
                    for part in (act_hi, act_lo):
                        for ch in range(NCH):
                            if first and not seeded and part is act_hi:
                                pe.wait_ge(bank_free, 4 * group + t * NCH + ch + 1)
                            nc.tensor.matmul(U[:, t * NCH + ch], part[:, tile, t * P:(t + 1) * P],
                                             hi[:, ch * 512:(ch + 1) * 512],
                                             start=first and not seeded and part is act_hi, stop=False)
                pe.wait_ge(lo_ready, count + 1)
                for t in range(TT):
                    for ch in range(NCH):
                        m = nc.tensor.matmul(U[:, t * NCH + ch], act_hi[:, tile, t * P:(t + 1) * P],
                                             lo[:, ch * 512:(ch + 1) * 512], start=False, stop=False)
                        if t == 0 and ch == 0:
                            m.then_inc(hi_slot_free, 1)
                m.then_inc(lo_slot_free, 1)

            pe.wait_ge(consts_ready, 1)
            pe.wait_ge(params_landed, 16 * 10)
            nc.tensor.transpose(X[0][:, 0:P], param_rows, ident[:])
            nc.tensor.transpose(X[0][:, P:2 * P], param_rows2, ident[:]).then_inc(params_ps, 1)
            pe.wait_ge(taps_landed, 16)
            for ct in range(CT):
                m = nc.tensor.transpose(X[1][:, ct * TAPS:(ct + 1) * TAPS], tap_rows[0:TAPS, ct * P:(ct + 1) * P],
                                        ident[0:TAPS, 0:TAPS])
            m.then_inc(params_ps, 1)
            pe.wait_ge(params_sb, 2)

            def mod_sums(b):
                pe.wait_ge(item_summed, KT * (b + 1))
                for s in range(2):
                    for j in range(BK):
                        m = nc.tensor.matmul(X[3][:, s * BK + j:s * BK + j + 1],
                                             wide[:, s * GC + j * P:s * GC + (j + 1) * P], ones[:, 0:1],
                                             start=True, stop=True)
                m.then_inc(mod_summed, 1)

            def x_transpose(b, q):
                if q == 0:
                    pe.wait_ge(x_scaled, 2 * (b + 1))
                if q == 3:
                    pe.wait_ge(h_ready, b * (BK // 2) + 1)
                for kk in range(2):
                    for t in range(TT):
                        k = 2 * q + kk
                        m = nc.tensor.transpose(X[q % 3][:, kk * T + t * P:kk * T + (t + 1) * P],
                                                x_block[b][:, t, k * P:(k + 1) * P], ident[:])
                m.then_inc(xT_ps, 1)

            def two_groups(b, it, after):
                for k in range(GROUPS_PER_BODY * BK):
                    k_tile(b * BK + k % BK, AG * BK * b + it * (GROUPS_PER_BODY * BK) + k, k,
                           AG * b + it * GROUPS_PER_BODY + k // BK, first=k % BK == 0, last=k % BK == BK - 1)
                    for step, *which in after.get(k, ()):
                        step(b + 1, *which)

            for q in range(3):
                x_transpose(0, q)
            mod_sums(0)
            x_transpose(0, 3)
            for b in range(NB):
                pe.wait_ge(act_lo_ready, (b + 1) * (BK // 2))
                pe.wait_ge(act_hi_ready, (b + 1) * (BK // 2))
                with pe.Fori(0, BODIES) as it:
                    two_groups(b, it, {})
                two_groups(b, BODIES, {} if b == NB - 1 else {
                    9: [(x_transpose, 0)], 10: [(x_transpose, 1)], 11: [(x_transpose, 2), (mod_sums,)],
                    13: [(x_transpose, 3)]})

            def gate_columns(n, ps, column):
                pe.wait_ge(item_summed, SUM_LAST + GATE_ITEMS * (n + 1))
                for j in range(GC // P):
                    m = nc.tensor.matmul(ps[:, j:j + 1], column(j), ones[:, 0:1], start=True, stop=True)
                m.then_inc(gcol_ps, 1)

            def glu_transpose(r):
                if r == 0:
                    pe.wait_ge(glu_ready, 4)
                if r >= 2:
                    pe.wait_ge(gluT_sb, r - 1)
                for kk in range(2):
                    ct = 2 * r + kk
                    for t in range(TT):
                        m = nc.tensor.transpose(X[r % 2][:, kk * T + t * P:kk * T + (t + 1) * P],
                                                ubuf[:, ct // 8, t, ct % 8 * P:(ct % 8 + 1) * P], ident[:])
                m.then_inc(gluT_ps, 1)

            def attend(step, h, local):
                if step == "transpose":
                    pe.wait_ge(qk_scaled, h + 1)
                    pe.wait_ge(qkT_sb, ONE + h)
                    for s in range(2):
                        for t in range(TT):
                            m = nc.tensor.transpose(X[3][:, s * T + t * P:s * T + (t + 1) * P],
                                                    pair[:, t, (2 * s + local) * HD:(2 * s + local + 1) * HD], ident[:])
                    m.then_inc(qkT_ps, 1)
                if step == "z":
                    pe.wait_ge(qkT_sb, ONE + h + 1)
                    pe.wait_ge(w_ready, ONE + h)
                    nc.tensor.matmul(X[1][:, 0:T], qkT[:, 1, 0:P], qkT[:, 0, :], start=True, stop=False,
                                     skip_group_check=True)
                    nc.tensor.matmul(X[1][:, T:T + P], qkT[:, 1, P:T], qkT[:, 0, P:T], start=False, stop=False,
                                     skip_group_check=True)
                    for diagonal in (0, T):
                        m = nc.tensor.matmul(X[1][:, diagonal:diagonal + P], ident_b[:], never[:], start=False,
                                             stop=False, skip_group_check=True)
                    m.then_inc(z_ps, 1)
                if step == "sum":
                    pe.wait_ge(soft_ready, h + 1)
                    nc.tensor.matmul(X[1][:, 0:T], neg_tri[:], absz[:, 0:T], start=False, stop=False,
                                     skip_group_check=True)
                    nc.tensor.matmul(X[1][:, P:T], neg_ones[:], absz[:, T:T + P], start=False, stop=False,
                                     skip_group_check=True)
                    nc.tensor.matmul(X[1][:, T:T + P], neg_tri[:], absz[:, T:T + P], start=False, stop=True,
                                     skip_group_check=True).then_inc(logw_ps, 1)
                if step == "o":
                    v = (4 + local) * HD
                    pe.wait_ge(w_ready, ONE + h + 1)
                    pe.wait_ge(y_done, ONE + h)
                    nc.tensor.matmul(X[2][:, 0:P], wexp[:, 0:P], pair[:, 0, v:v + HD], start=True, stop=True)
                    nc.tensor.matmul(X[2][:, P:T], wexp[:, P:T], pair[:, 0, v:v + HD], start=False, stop=False,
                                     skip_group_check=True)
                    nc.tensor.matmul(X[2][:, P:T], wexp[:, T:T + P], pair[:, 1, v:v + HD], start=False, stop=True,
                                     skip_group_check=True).then_inc(o_ps, 1)

            PE_STEPS = {8: ("transpose", 0), 10: ("z", 0), 14: ("sum", 0), 16: ("transpose", 1), 17: ("o", 0),
                        19: ("z", 1), 23: ("sum", 1), 26: ("o", 1)}
            for k in range(KT):
                k_tile(k, TILE_B + k, k, GROUP_B, first=k == 0, last=k == KT - 1)
                if 4 <= k < 4 + CT // 2:
                    glu_transpose(k - 4)
                if k == 3:
                    gate_columns(0, X[3], lambda j: gate_sum0[:, j * P:(j + 1) * P])
            pe.wait_ge(gcol_ready, 1)
            with pe.Fori(1, PAIRS - 1) as g:
                for k in range(KT):
                    k_tile(k, TILE_B + g * KT + k, k, GROUP_B + g, first=k == 0, last=k == KT - 1)
                    if k in PE_STEPS:
                        step, local = PE_STEPS[k]
                        attend(step, (g - 1) * 2 + local, local)

            def channel_sums(n, source, weights, seen, ready):
                pe.wait_ge(*seen)
                for ct in range(4 * n, 4 * n + 4):
                    m = nc.tensor.matmul(X[0][:, 0:T], weights[:], source[:, ct], start=ct == 0, stop=ct == CT - 1)
                if n == CT // 4 - 1:
                    m.then_inc(ready, 1)

            g = PAIRS - 1
            pe.wait_ge(gluT_sb, CT // 2)
            for k in range(KT):
                k_tile(k, TILE_B + g * KT + k, k, GROUP_B + g, first=k == 0, last=k == KT - 1)
                if k in PE_STEPS:
                    step, local = PE_STEPS[k]
                    attend(step, (g - 1) * 2 + local, local)
                if k == 5:
                    gate_columns(1, X[3], lambda j: gate_sum1[:, j // 4, j % 4 * P:(j % 4 + 1) * P])
                if k == 7:
                    pe.wait_ge(gcol_ready, 2)
                if 1 <= k <= 4:
                    channel_sums(k - 1, conv_out, neg_ones, (conv_step, CT * TAPS), mean_ps)
                if k == 12:
                    pe.wait_ge(xc_ready, 1)
                if 12 <= k <= 15:
                    channel_sums(k - 12, conv_in, ones, (sqc_ready, k - 12 + 1), var_ps)

            def y_transpose(r, bank, source, ready):
                for kk in range(2):
                    for t in range(TT):
                        m = nc.tensor.transpose(bank[:, kk * T + t * P:kk * T + (t + 1) * P],
                                                source(2 * r + kk, t), ident[:])
                m.then_inc(ready, 1)

            def sb_source(kt, t):
                return ysb[:, t, kt * P:(kt + 1) * P]

            def conv_source(kt, t):
                return gatebuf[:, kt // 8, t, kt % 8 * P:(kt % 8 + 1) * P]

            pe.wait_ge(bpw_landed, 16)
            pe.wait_ge(var_ready, 1)
            for s in range(PG * PKT):
                g, k = s // PKT, s % PKT
                if k == 0:
                    for t in range(TT):
                        for ch in range(NCH):
                            pe.wait_ge(bank_free, 4 * (GROUP_P + g) + t * NCH + ch + 1)
                            nc.tensor.matmul(U[:, t * NCH + ch], ones[0:1, :],
                                             bias_row[:, g * GC + ch * 512:g * GC + (ch + 1) * 512], start=True, stop=False)
                if g == 0:
                    pe.wait_ge(conv_lo, k // 2 + 1)
                k_tile(k, TILE_P + s, s, last=k == PKT - 1, first=k == 0, seeded=True)
                if s in PE_STEPS:
                    step, local = PE_STEPS[s]
                    attend(step, (PAIRS - 1) * 2 + local, local)
                if s in SB_ROUNDS:
                    r = SB_ROUNDS.index(s)
                    pe.wait_ge(y_done, ONE + 2 * (r + 1))
                    if r:
                        pe.wait_ge(ysb_lo, r)
                    y_transpose(r, X[0], sb_source, ysbT_ps)
            pe.wait_ge(y_done, ONE + 2 * PAIRS)
            pe.wait_ge(w_ready, ONE + 2 * PAIRS)
            pe.wait_ge(bank_free, 4 * (GROUP_P + PG) + 4)

            def out_group(g, after):
                for k in range(KT):
                    k_tile((k + KT // 2) % KT, TILE_O + g * KT + k, k, GROUP_O + g, first=k == 0, last=k == KT - 1)
                    if k == KT - 3:
                        pe.wait_ge(diag_ready, g + 1)
                        pe.wait_ge(gate_ready, ONE + 2 * g)
                        for ch in range(NCH):
                            m = nc.tensor.matmul(X[2 + ch][:], ones[:], gate_diag[:, 4 * ch:4 * ch + 4, :],
                                                 start=True, stop=True)
                        m.then_inc(gate_ps, 1)
                    after(k)

            def first_group(k):
                if k in LATE_ROUNDS:
                    n = LATE_ROUNDS.index(k)
                    if n == 0:
                        pe.wait_ge(ysb_lo, CT // 2 - 1)
                        y_transpose(CT // 2 - 1, X[0], sb_source, ysbT_ps)
                    else:
                        if n == 2:
                            pe.wait_ge(ysb_lo, CT // 2)
                        if n > 2:
                            pe.wait_ge(yc_lo, n - 2)
                        y_transpose(n - 1, X[n % 2], conv_source, ycT_ps)
                if k == 13:
                    pe.wait_ge(ysb_lo, CT // 2)
                if k >= KT // 2 - 1 and k % 2 == 1 and k < KT - 1:
                    pe.wait_ge(yc_lo, (k - KT // 2 + 1) // 2 + 1)
                if k == KT - 4:
                    gate_columns(2, X[0], lambda j: gate_sum[:, j * P:(j + 1) * P])

            out_group(0, first_group)
            with pe.Fori(1, OG - 1) as g:
                out_group(g, lambda k: None)
            pe.wait_ge(gcol_ready, 3)
            out_group(OG - 1, lambda k: gate_columns(3, X[0], lambda j: gate_sum[:, j * P:(j + 1) * P]) if k == 1 else None)

        @block.scalar
        def _(act):
            def copy(dst, src):
                return nc.scalar.activation(dst, src, ACT.Copy)

            def high(count, slot, item_slot, kk, lands):
                act.wait_ge(raw_landed[item_slot], lands)
                act.wait_ge(hi_slot_free, count + 1)
                copy(whi[:, slot % HI], raw[:, item_slot, kk]).then_inc(hi_ready, 1)

            for s in (qkT_sb, w_ready, gate_ready):
                act.sem_inc(s, ONE)

            act.wait_ge(pool_step, 1)
            for n, v in enumerate((c[0], norm_g[0], b_ada[0, 0:D], b_ada[0, D:2 * D])):
                act.dma_start(param_rows[n * KT:(n + 1) * KT, :], v.rearrange("(k p) -> k p", p=P)).then_inc(params_landed, 16)
            for n, v in enumerate((ln_g[0], ln_b[0], b_dw[0])):
                act.dma_start(param_rows2[n * CT:(n + 1) * CT, :], v.rearrange("(k p) -> k p", p=P)).then_inc(params_landed, 16)
            act.dma_start(param_rows2[3 * CT:3 * CT + 1, :], q_norm_g).then_inc(params_landed, 16)
            act.dma_start(param_rows2[3 * CT + 1:3 * CT + 2, :], k_norm_g).then_inc(params_landed, 16)
            act.dma_start(param_rows2[3 * CT + 2:3 * CT + 2 + KT, :],
                          b_ada[0, 2 * D:3 * D].rearrange("(k p) -> k p", p=P)).then_inc(params_landed, 16)
            act.dma_start(tap_rows[0:TAPS, :], w_dw[0]).then_inc(taps_landed, 16)
            act.wait_ge(params_sb, 1)
            nc.scalar.activation(silu_c[:], cols[:, 0], ACT.Silu).then_inc(silu_ready, 1)
            act.wait_ge(ms_ready, 1)
            nc.scalar.activation(x_rms, x_ms, ACT.Sqrt).then_inc(rms_ready, 1)

            def x_scale(b):
                act.wait_ge(x_landed[b], 16)
                for t in range(TT):
                    nc.scalar.activation(x_block[b][:, t], x_block[b][:, t], ACT.Copy,
                                         scale=x_rstd[:, t:t + 1]).then_inc(x_scaled, 1)

            def x_high(b, q):
                act.wait_ge(h_ready, b * (BK // 2) + q + 1)
                copy(act_hi[:, b * BK + 2 * q:b * BK + 2 * q + 2], h32[:, q % 2]).then_inc(act_hi_ready, 1)

            def two_groups(b, kinds, it, body_items):
                k = 0
                for n, kind in enumerate(kinds):
                    if kind == "w":
                        for kk in range(2):
                            high(AG * BK * b + it * (GROUPS_PER_BODY * BK) + k, k, n % SLOTS, kk,
                                 landed(ITEM_A + b * BLOCK_ITEMS + n) + it * (body_items // SLOTS * 16))
                            k += 1

            act.wait_ge(rstd_ready, 1)
            x_scale(0)
            for q in range(BK // 2):
                x_high(0, q)
            for b in range(NB):
                body, end = (items_of(LAST_BODY), items_of(LAST_END)) if b == NB - 1 else (items_of(BODY), items_of(END))
                with act.Fori(0, BODIES) as it:
                    two_groups(b, body, it, len(body))
                if b < NB - 1:
                    x_scale(b + 1)
                two_groups(b, end, BODIES, len(body))
                if b < NB - 1:
                    for q in range(BK // 2):
                        x_high(b + 1, q)

            PAIR_ITEM = [n for n, kind in enumerate(PAIR_BODY) if kind == "w"]

            def pair_tile(g, k, lands, item=None):
                n = k // 2 if item is None else item[k // 2]
                high(TILE_B + g * KT + k, k, n % SLOTS, k % 2, lands(g, n))

            def prepare_pair(step, g):
                if step == "squares":
                    act.wait_ge(bank_free, 4 * (GROUP_B + g + 1) + 4)
                    act.wait_ge(hstat_ready, ONE + g)
                    act.wait_ge(o_ps, ONE + 2 * g)
                    for t in range(TT):
                        for j in range(4):
                            i = nc.scalar.activation(squares[:, t * 4 + j], pair[:, t, j * HD:(j + 1) * HD], ACT.Square,
                                                     accum_out=hstat[:, 0, t * 4 + j:t * 4 + j + 1])
                            i.then_inc(sq_ready, 1)
                if step == "roots":
                    act.wait_ge(hstat_dve, 4 * g + 1)
                    nc.scalar.activation(hstat[:, 1], hstat[:, 0], ACT.Ln).then_inc(hstat_act, 1)
                    act.wait_ge(hstat_act, 2 * g + 1)
                    nc.scalar.activation(hstat[:, 1], hstat[:, 1], ACT.Exp, scale=-0.5).then_inc(hstat_act, 1)
                if step == "gate":
                    act.wait_ge(y_done, ONE + 2 * g)
                    nc.scalar.activation(sig[:], pair[:, :, 6 * HD:8 * HD], ACT.Silu).then_inc(sig_ready, 1)

            def attend(step, h, local):
                if step == "scale":
                    for t in range(TT):
                        for s in range(2):
                            j = 2 * s + local
                            seg = pair[:, t, j * HD:(j + 1) * HD]
                            i = nc.scalar.activation(seg, seg, ACT.Copy, scale=hstat[:, 2, t * 4 + j:t * 4 + j + 1])
                    i.then_inc(qk_scaled, 1)
                if step == "gains":
                    act.wait_ge(qkT_ps, h + 1)
                    act.wait_ge(z_ps, ONE + h)
                    nc.scalar.activation(qkT[:, 0], X[3][:, 0:T], ACT.Copy, scale=cols2[:, 3 * CT:3 * CT + 1])
                    nc.scalar.activation(qkT[:, 1], X[3][:, T:2 * T], ACT.Copy,
                                         scale=cols2[:, 3 * CT + 1:3 * CT + 2]).then_inc(qkT_sb, 1)
                if step == "soft":
                    act.wait_ge(z_ps, ONE + h + 1)
                    act.wait_ge(logw_ps, ONE + h)
                    nc.scalar.activation(absz, X[1][:, 0:3 * P], ACT.Abs).then_inc(abs_ready, 1)
                    act.wait_ge(abs_ready, h + 1)
                    nc.scalar.activation(absz[:], absz[:], ACT.Exp, scale=-1.0).then_inc(exp_ready, 1)
                    act.wait_ge(exp_ready, h + 1)
                    nc.scalar.activation(absz[:], absz[:], ACT.Ln, bias=1.0).then_inc(log_ready, 1)
                if step == "w":
                    act.wait_ge(logw_ps, ONE + h + 1)
                    act.wait_ge(o_ps, ONE + h)
                    nc.scalar.activation(wexp[:], X[1][:, 0:3 * P], ACT.Exp).then_inc(w_ready, 1)

            ACT_PREP = {4: "squares", 5: "roots", 6: "gate"}
            ACT_STEPS = {8: ("scale", 0), 12: ("gains", 0), 10: ("scale", 1), 15: ("soft", 0), 18: ("w", 0),
                         20: ("gains", 1), 24: ("soft", 1), 27: ("w", 1)}

            def glu_gates(n):
                if n < 4:
                    piece = glubuf[:, n // 2, n % 2]
                    nc.scalar.activation(piece, piece, ACT.Sigmoid).then_inc(gates_ready, 1)
                else:
                    piece = gatebuf[:, n // 2 - 2, n % 2]
                    nc.scalar.activation(piece, piece, ACT.Silu).then_inc(gates_ready, 1)

            for k in range(KT):
                pair_tile(0, k, landed_first)
                if k == 0:
                    act.wait_ge(bank_free, 4 * GROUP_B + 4)
                if k < 8:
                    glu_gates(k)
                if 8 <= k < 8 + CT // 2:
                    r = k - 8
                    act.wait_ge(gluT_ps, r + 1)
                    copy(conv_in[:, 2 * r:2 * r + 2].rearrange("p c t -> p (c t)"), X[r % 2][:]).then_inc(gluT_sb, 1)
            def attend_at(k, p):
                if k in ACT_PREP:
                    prepare_pair(ACT_PREP[k], p)
                if k in ACT_STEPS:
                    step, local = ACT_STEPS[k]
                    if step == "scale":
                        act.wait_ge(hstat_ready, ONE + p + 1)
                    attend(step, p * 2 + local, local)

            with act.Fori(1, LOOP1_END) as g:
                for k in range(KT):
                    pair_tile(g, k, landed_loop1)
                    attend_at(k, g - 1)
            with act.Fori(LOOP1_END, PAIRS - 1) as g:
                for k in range(KT):
                    pair_tile(g, k, landed_loop2, PAIR_ITEM)
                    attend_at(k, g - 1)

            SQUARES = {13: 0, 14: 1, 16: 2, 17: 3}
            SWISH = {26: 0, 28: 1, 29: 2, 30: 3}
            for k in range(KT):
                pair_tile(PAIRS - 1, k, landed_last)
                attend_at(k, PAIRS - 2)
                if k in SQUARES:
                    n = SQUARES[k]
                    act.wait_ge(xc_ready, n + 2)
                    nc.scalar.activation(conv_in[:, 4 * n:4 * n + 4], conv_out[:, 4 * n:4 * n + 4], ACT.Square).then_inc(sqc_ready, 1)
                if k == 21:
                    act.wait_ge(var_ready, 1)
                    nc.scalar.activation(ln_stat[:], ln_stat[:], ACT.Sqrt).then_inc(deviation_ready, 1)
                if k in SWISH:
                    n = SWISH[k]
                    act.wait_ge(norm_ready, n + 1)
                    for ct in range(4 * n, 4 * n + 4):
                        nc.scalar.activation(conv_out[:, ct], conv_out[:, ct], ACT.Silu, scale=cols2[:, ct:ct + 1],
                                             bias=cols2[:, CT + ct:CT + ct + 1]).then_inc(swish_ready, 1)

            def y_high(r, bank, ps, ready, tile):
                act.wait_ge(ps, r + 1)
                copy(act_hi[:, tile:tile + 2].rearrange("p c t -> p (c t)"), bank[:]).then_inc(ready, 1)

            weight_items = [n for n, kind in enumerate(P_ITEMS) if kind == "w"]
            for s in range(PG * PKT):
                n = weight_items[s // 2]
                high(TILE_P + s, s, n % SLOTS, s % 2, landed(ITEM_P + n) + EXTRA)
                if s == 3:
                    act.wait_ge(lo_slot_free, TILE_P + LO)
                for r in {3: (0, 1)}.get(s, (s - 2,) if 4 <= s < 2 + CT // 2 else ()):
                    act.wait_ge(swish_ready, 2 * r + 2)
                    copy(act_hi[:, 2 * r:2 * r + 2], conv_out[:, 2 * r:2 * r + 2]).then_inc(conv_hi, 1)
                attend_at(s, PAIRS - 1)
                if s - 4 in SB_ROUNDS:
                    r = SB_ROUNDS.index(s - 4)
                    y_high(r, X[0], ysbT_ps, ysb_hi, KT // 2 + 2 * r)

            def out_high(g, k, item, kinds):
                n = [n for n, kind in enumerate(kinds) if kind == "w"][k // 2]
                high(TILE_O + g * KT + k, k, n % SLOTS, k % 2, landed(item + n) + EXTRA)

            def spread_gate(g):
                act.wait_ge(gate_ps, ONE + g + 1)
                act.wait_ge(bank_free, 4 * (GROUP_O + g) + 4)
                for ch in range(NCH):
                    copy(gate_sb[:, ch * 512:(ch + 1) * 512], X[2 + ch][:]).then_inc(gate_ready, 1)

            for k in range(KT):
                out_high(0, k, ITEM_O, O_BODY)
                if k - 4 in LATE_ROUNDS:
                    n = LATE_ROUNDS.index(k - 4)
                    if n == 0:
                        y_high(CT // 2 - 1, X[0], ysbT_ps, ysb_hi, KT - 2)
                        act.wait_ge(bank_free, 4 * (GROUP_P + PG) + 4)
                    else:
                        y_high(n - 1, X[n % 2], ycT_ps, yc_hi, 2 * (n - 1))
            spread_gate(0)
            weight_items = [n for n, kind in enumerate(O_BODY) if kind == "w"]
            with act.Fori(1, OG - 1) as g:
                for k in range(KT):
                    n = weight_items[k // 2]
                    high(TILE_O + g * KT + k, k, n % SLOTS, k % 2,
                         landed(ITEM_O1 + n) + EXTRA + (g - 1) * (len(O_BODY) // SLOTS * 16))
                spread_gate(g)
            for k in range(KT):
                out_high(OG - 1, k, ITEM_O3, O_LAST)
            spread_gate(OG - 1)

        @block.gpsimd
        def _(pool):
            nc.gpsimd.memset(param_rows2, 0.0).then_inc(pool_step, 1)
            for n, (dst, value) in enumerate(((ident, 0.0), (neg_tri, -1.0), (neg_ones, -1.0), (ones, 1.0), (never, 0.0), (ident_b, 0.0))):
                nc.gpsimd.memset(dst[:], value).then_inc(pool_step, 1)
            pool.wait_ge(pool_step, 7)
            nc.gpsimd.affine_select(out=ident[:], in_=ident[:], compare_op=ALU.not_equal, fill=1.0, base=0,
                                    pattern=[[-1, P]], channel_multiplier=1).then_inc(pool_step, 1)
            nc.gpsimd.affine_select(out=neg_tri[:], in_=neg_tri[:], compare_op=ALU.is_ge, fill=0.0, base=0,
                                    pattern=[[-1, P]], channel_multiplier=1).then_inc(pool_step, 1)
            nc.gpsimd.affine_select(out=never[:], in_=never[:], compare_op=ALU.is_gt, fill=NEVER, base=0,
                                    pattern=[[1, P]], channel_multiplier=-1).then_inc(pool_step, 1)
            nc.gpsimd.affine_select(out=ident_b[:], in_=ident_b[:], compare_op=ALU.not_equal, fill=1.0, base=0,
                                    pattern=[[-1, P]], channel_multiplier=1).then_inc(pool_step, 1)
            pool.wait_ge(pool_step, 11)
            nc.gpsimd.memset(wide[:], 0.0).then_inc(wide_zeroed, 1)
            pool.wait_ge(wide_zeroed, 1)
            pool.sem_inc(consts_ready, 1)
            for b in range(NB):
                pool.wait_ge(mod_summed, b + 1)
                nc.gpsimd.memset(wide[:], 0.0).then_inc(wide_zeroed, 1)

            pool.wait_ge(xT_ps, KT // 2)
            nc.gpsimd.memset(gate_sum1, 0.0).then_inc(gate_zeroed, 1)
            pool.wait_ge(var_ps, 1)
            pool.dma_start(bias_row, b_pw).then_inc(bpw_landed, 16)
            nc.gpsimd.memset(gate_sum, 0.0).then_inc(gate_zeroed, 1)
            pool.wait_ge(conv_lo, CT // 2)
            for g in range(OG):
                pool.wait_ge(out_ready, TT * g)
                pool.dma_start(x_res, x[0].rearrange("(t p) (g n) -> g p t n", p=P, n=GC)[g]).then_inc(xres_landed, 16)
                if g == 0:
                    pool.wait_ge(gcol_ps, 3)
                    nc.gpsimd.memset(gate_sum, 0.0).then_inc(gate_zeroed, 1)
                for t in range(TT):
                    pool.wait_ge(out_ready, TT * g + t + 1)
                    pool.dma_start(out_rows[g][:, t], y_out[:, t]).then_inc(stored, 16)
                pool.wait_ge(stored, 16 * TT * (g + 1))
                pool.sem_inc(y_out_free, 1)

        @block.vector
        def _(dve):
            dve.sem_inc(bank_free, 4)
            for s in (y_done, hstat_ready):
                dve.sem_inc(s, ONE)
            dve.sem_inc(y_out_free, ONE)
            steps = [0]

            def then(instruction):
                steps[0] += 1
                instruction.then_inc(dve_step, 1)
                dve.wait_ge(dve_step, steps[0])

            def low(count, slot, item_slot, kk):
                dve.wait_ge(hi_ready, count + 1)
                dve.wait_ge(lo_slot_free, count + 1)
                nc.vector.tensor_tensor(wlo[:, slot % LO], raw[:, item_slot, kk],
                                        whi[:, slot % HI].bitcast(F32), ALU.subtract).then_inc(lo_ready, 1)

            def x_squares(b):
                dve.wait_ge(x_landed[b], 16)
                for t in range(TT):
                    if b >= 2:
                        dve.wait_ge(x_squared, (b - 2) * TT + t + 1)
                    nc.vector.tensor_tensor_reduce(out=cbuf[:, b % 2, t], in0=x_block[b][:, t], in1=x_block[b][:, t],
                                                   scale=1.0, scalar=0.0, op0=ALU.mult, op1=ALU.add,
                                                   accum_out=x_sums[:, t, b:b + 1]).then_inc(x_squared, 1)

            x_squares(0)
            dve.wait_ge(params_ps, 1)
            nc.vector.tensor_copy(cols[:].rearrange("p a k -> p (a k)"), X[0][:, 0:P])
            then(nc.vector.tensor_copy(cols2[:], X[0][:, P:P + 3 * CT + 2 + KT]))
            nc.vector.tensor_scalar(cols2[:, 3 * CT:3 * CT + 1], cols2[:, 3 * CT:3 * CT + 1], HD ** -0.5, None,
                                    ALU.mult).then_inc(params_sb, 1)
            dve.wait_ge(params_ps, 2)
            nc.vector.tensor_copy(taps[:].rearrange("p c k -> p (c k)"), X[1][:, 0:CT * TAPS]).then_inc(params_sb, 1)
            for b in range(1, NB):
                x_squares(b)
            dve.wait_ge(x_squared, NB * TT)
            then(nc.vector.tensor_tensor(x_pair_sums, x_sums[:, :, 0:2], x_sums[:, :, 2:4], ALU.add))
            then(nc.vector.tensor_tensor(x_ms, x_pair_sums[:, :, 0], x_pair_sums[:, :, 1], ALU.add))
            nc.vector.tensor_scalar(x_ms, x_ms, 1.0 / D, EPS, ALU.mult, ALU.add).then_inc(ms_ready, 1)
            dve.wait_ge(rms_ready, 1)
            nc.vector.reciprocal(x_rstd, x_rms).then_inc(rstd_ready, 1)
            dve.wait_ge(silu_ready, 1)
            dve.wait_ge(wide_zeroed, 1)

            def ada(k, item_slot, lands, summed):
                dve.wait_ge(raw_landed[item_slot], lands)
                if not isinstance(summed, int) or summed:
                    dve.wait_ge(item_summed, summed)
                nc.vector.scalar_tensor_tensor(out=wide[:], in0=raw[:, item_slot].rearrange("p a n -> p (a n)"),
                                               scalar=k, in1=wide[:], op0=ALU.mult, op1=ALU.add).then_inc(item_summed, 1)

            for k in range(KT):
                n = k
                ada(silu_c[:, k:k + 1], n % SLOTS, landed(n), n)

            def gate_item(sums, k, item_slot, lands, done):
                dve.wait_ge(raw_landed[item_slot], lands)
                for kk, (before, count, signal) in enumerate((
                        (item_summed, SUM_LAST + done, gate_step), (gate_step, done + 1, item_summed))):
                    part = raw[:, item_slot, kk]
                    if len(sums.shape) == 3:
                        part = part.rearrange("p (t n) -> p t n", t=TT)
                    dve.wait_ge(before, count)
                    nc.vector.scalar_tensor_tensor(out=sums, in0=part, scalar=silu_c[:, bass.ds(k + kk, 1)],
                                                   in1=sums, op0=ALU.mult, op1=ALU.add).then_inc(signal, 1)

            def gate_column(n, ps):
                dve.wait_ge(gcol_ps, n + 1)
                bias = cols2[:, 3 * CT + 2:].rearrange("p (g j) -> p g j", g=OG)
                nc.vector.tensor_tensor(gate_cols[:, n], ps[:, 0:GC // P], bias[:, n], ALU.add).then_inc(gcol_ready, 1)

            def mod_columns(b):
                dve.wait_ge(mod_summed, b + 1)
                ks = slice(b * BK, (b + 1) * BK)
                nc.vector.tensor_tensor(mod_add[:], X[3][:, 0:BK], cols[:, 2, ks], ALU.add)
                then(nc.vector.tensor_tensor(mod_mul[:], X[3][:, BK:2 * BK], cols[:, 3, ks], ALU.add))
                then(nc.vector.scalar_tensor_tensor(out=mod_mul[:], in0=mod_mul[:], scalar=1.0, in1=cols[:, 1, ks],
                                                    op0=ALU.add, op1=ALU.mult))

            def affine(b, q):
                n = b * (BK // 2) + q
                dve.wait_ge(xT_ps, n + 1)
                if n >= 2:
                    dve.wait_ge(act_hi_ready, n - 1)
                    dve.wait_ge(act_lo_ready, n - 1)
                for kk in range(2):
                    k = 2 * q + kk
                    i = nc.vector.tensor_scalar(h32[:, q % 2, kk], X[q % 3][:, kk * T:(kk + 1) * T],
                                                mod_mul[:, k:k + 1], mod_add[:, k:k + 1], ALU.mult, ALU.add)
                i.then_inc(h_ready, 1)

            def x_low(b, q):
                dve.wait_ge(act_hi_ready, b * (BK // 2) + q + 1)
                dve.wait_ge(h_ready, b * (BK // 2) + q + 1)
                ks = slice(b * BK + 2 * q, b * BK + 2 * q + 2)
                nc.vector.tensor_tensor(act_lo[:, ks], h32[:, q % 2], act_hi[:, ks].bitcast(F32),
                                        ALU.subtract).then_inc(act_lo_ready, 1)

            def two_groups(b, kinds, it, after):
                body_items = len(items_of(LAST_BODY if b == NB - 1 else BODY))
                n = k = a_items = 0
                for kind in kinds:
                    group = AG * b + it * GROUPS_PER_BODY + (k - 1) // BK
                    lands = landed(ITEM_A + b * BLOCK_ITEMS + n) + it * (body_items // SLOTS * 16)
                    if kind == "w":
                        for kk in range(2):
                            if k % BK:
                                low(AG * BK * b + it * (GROUPS_PER_BODY * BK) + k, k, n % SLOTS, kk)
                            for step, *which in after.get(k, ()):
                                step(b + 1, *which)
                            k += 1
                        n += 1
                    elif kind == "a" and b == NB - 1:
                        done = it * LAST_BODY.count("a") + a_items
                        gate_item(gate_sum0, done * 2, n % SLOTS, lands, done)
                        a_items += 1
                        n += 1
                    elif kind == "a":
                        kt = it * A_PER_BODY + a_items
                        ada(silu_c[:, bass.ds(kt, 1)], n % SLOTS, lands, SUM_A + KT * b + kt)
                        a_items += 1
                        n += 1
                    else:
                        low(AG * BK * b + it * (GROUPS_PER_BODY * BK) + k, 0, n % SLOTS, 0)
                        for t in range(TT):
                            if t == 0:
                                dve.wait_ge(half_done, group + 1)
                            else:
                                dve.wait_ge(lo_slot_free, AG * BK * b + it * (GROUPS_PER_BODY * BK) + k + LO)
                            for ch in range(NCH):
                                dst = cbuf[:, it * GROUPS_PER_BODY + (k - 1) // BK, t, ch * 512:(ch + 1) * 512]
                                if b == 0:
                                    nc.vector.tensor_copy(dst, U[:, t * NCH + ch]).then_inc(bank_free, 1)
                                else:
                                    nc.vector.tensor_tensor(dst, dst, U[:, t * NCH + ch], ALU.add).then_inc(bank_free, 1)

            mod_columns(0)
            for q in range(BK // 2):
                affine(0, q)
                if q:
                    x_low(0, q - 1)
            x_low(0, BK // 2 - 1)
            low(0, 0, 0, 0)
            for b in range(NB):
                dve.wait_ge(wide_zeroed, b + 2)
                with dve.Fori(0, BODIES) as it:
                    two_groups(b, LAST_BODY if b == NB - 1 else BODY, it, {})
                two_groups(b, LAST_END if b == NB - 1 else END, BODIES, {} if b == NB - 1 else {
                    13: [(mod_columns,), (affine, 0), (affine, 1)],
                    14: [(x_low, 0), (affine, 2)],
                    15: [(x_low, 1), (affine, 3), (x_low, 2), (x_low, 3)]})

            def empty_group(group, tiles, place, next_slot=0):
                if next_slot is not None:
                    low(tiles, 0, next_slot, 0)
                for t in range(TT):
                    if t == 0:
                        dve.wait_ge(half_done, group + 1)
                    else:
                        dve.wait_ge(lo_slot_free, tiles + LO)
                    for ch in range(NCH):
                        place(U[:, t * NCH + ch], t, slice(ch * 512, (ch + 1) * 512)).then_inc(bank_free, 1)

            def conv_tap(tiles, first_tile, taps_before, n):
                a, shift = n % tiles, n // tiles
                ct = first_tile + a
                weight = taps[:, ct, TAPS - 1 - shift:TAPS - shift]
                if shift == 0:
                    nc.vector.tensor_scalar(conv_out[:, ct, :], conv_in[:, ct, :], weight,
                                            cols2[:, bass.ds(2 * CT + ct, 1)], ALU.mult, ALU.add).then_inc(conv_step, 1)
                else:
                    dve.wait_ge(conv_step, taps_before + n - tiles + 1)
                    nc.vector.scalar_tensor_tensor(out=conv_out[:, ct, shift:T], in0=conv_in[:, ct, 0:T - shift],
                                                   scalar=weight, in1=conv_out[:, ct, shift:T],
                                                   op0=ALU.mult, op1=ALU.add).then_inc(conv_step, 1)

            def prepare_pair(step, p):
                if step == "mean":
                    dve.wait_ge(sq_ready, 8 * (p + 1))
                    nc.vector.tensor_scalar(hstat[:, 0], hstat[:, 0], 1.0 / HD, EPS, ALU.mult, ALU.add).then_inc(hstat_dve, 1)
                if step == "newton":
                    dve.wait_ge(hstat_act, 2 * (p + 1))
                    nc.vector.tensor_tensor(hstat[:, 2], hstat[:, 1], hstat[:, 1], ALU.mult).then_inc(hstat_dve, 1)
                    dve.wait_ge(hstat_dve, 4 * p + 2)
                    nc.vector.tensor_tensor(hstat[:, 2], hstat[:, 2], hstat[:, 0], ALU.mult).then_inc(hstat_dve, 1)
                    dve.wait_ge(hstat_dve, 4 * p + 3)
                    nc.vector.tensor_scalar(hstat[:, 2], hstat[:, 2], -0.5, 1.5, ALU.mult, ALU.add).then_inc(hstat_dve, 1)
                    dve.wait_ge(hstat_dve, 4 * p + 4)
                    nc.vector.tensor_tensor(hstat[:, 2], hstat[:, 2], hstat[:, 1], ALU.mult).then_inc(hstat_ready, 1)

            def attend(step, p, local):
                h = 2 * p + local
                if step == "soft":
                    dve.wait_ge(log_ready, h + 1)
                    nc.vector.scalar_tensor_tensor(out=absz, in0=X[1][:, 0:3 * P], scalar=0.0, in1=absz,
                                                   op0=ALU.max, op1=ALU.add).then_inc(soft_ready, 1)
                if step == "y":
                    dve.wait_ge(o_ps, ONE + h + 1)
                    dve.wait_ge(sig_ready, p + 1)
                    nc.vector.tensor_tensor(ysb[:, :, bass.ds(h * HD, HD)], X[2][:, 0:T].rearrange("p (t d) -> p t d", t=TT),
                                            sig[:, :, local * HD:(local + 1) * HD], ALU.mult).then_inc(y_done, 1)

            DVE_PREP = {3: "mean", 4: "newton"}
            DVE_STEPS = {14: ("soft", 0), 19: ("y", 0), 23: ("soft", 1), 28: ("y", 1)}

            def attend_at(k, p):
                if k in DVE_PREP:
                    prepare_pair(DVE_PREP[k], p)
                if k in DVE_STEPS:
                    attend(DVE_STEPS[k][0], p, DVE_STEPS[k][1])

            def keep_pair(bank, t, columns):
                return nc.vector.tensor_copy(pair[:, t, columns], bank)

            PAIR_ITEM = [n for n, kind in enumerate(PAIR_BODY) if kind == "w"]

            def split_pair_tile(g, k, item=None):
                if k:
                    low(TILE_B + g * KT + k, k, (k // 2 if item is None else item[k // 2]) % SLOTS, k % 2)

            for k in range(KT):
                split_pair_tile(0, k)
                if k == 0:
                    dve.wait_ge(bank_free, 4 * GROUP_B + 4)
                if k == 8:
                    gate_column(0, X[3])
                if 1 <= k <= 4:
                    n = k - 1
                    dve.wait_ge(gates_ready, n + 1)
                    u, gate = ubuf[:, n // 2, n % 2], glubuf[:, n // 2, n % 2]
                    nc.vector.tensor_tensor(u, u, gate, ALU.mult).then_inc(glu_ready, 1)
                if k >= KT // 2:
                    if k == KT // 2:
                        dve.wait_ge(gluT_sb, CT // 2)
                    for n in range(4 * (k - KT // 2), min(4 * (k - KT // 2) + 4, CONV_FIRST * TAPS)):
                        conv_tap(CONV_FIRST, 0, 0, n)
            empty_group(GROUP_B, TILE_B + KT, keep_pair)
            def conv_taps(k, tiles, ct):
                if k >= KT - TAPS:
                    for n in range(tiles * (k - (KT - TAPS)), tiles * (k - (KT - TAPS) + 1)):
                        conv_tap(tiles, ct, ct * TAPS, n)

            with dve.Fori(1, LOOP1_END) as g:
                for k in range(KT):
                    split_pair_tile(g, k)
                    attend_at(k, g - 1)
                    conv_taps(k, CONV_LOOP1, CONV_FIRST + (g - 1) * CONV_LOOP1)
                empty_group(GROUP_B + g, TILE_B + g * KT + KT, keep_pair)
            dve.wait_ge(gate_zeroed, 1)
            with dve.Fori(LOOP1_END, PAIRS - 1) as g:
                k = a_items = 0
                for n, kind in enumerate(PAIR_BODY):
                    if kind == "a":
                        done = (g - LOOP1_END) * (GATE_ITEMS // 2) + a_items
                        gate_item(gate_sum1, 2 * done, n % SLOTS, landed_loop2(g, n), GATE_ITEMS + done)
                        a_items += 1
                        continue
                    for kk in range(2):
                        split_pair_tile(g, k, PAIR_ITEM)
                        attend_at(k, g - 1)
                        conv_taps(k, CONV_LOOP2, CONV_FIRST + (LOOP1_END - 1) * CONV_LOOP1 + (g - LOOP1_END) * CONV_LOOP2)
                        k += 1
                empty_group(GROUP_B + g, TILE_B + g * KT + KT, keep_pair)

            across = ln_stat[:].unsqueeze(1).to_broadcast([P, 4, T])
            for k in range(KT):
                split_pair_tile(PAIRS - 1, k)
                attend_at(k, PAIRS - 2)
                if k == 7:
                    gate_column(1, X[3])
                if k == 7:
                    dve.wait_ge(mean_ps, 1)
                    nc.vector.tensor_scalar(ln_stat[:], X[0][:, 0:T], 1.0 / CW, None, ALU.mult).then_inc(xc_ready, 1)
                if 8 <= k <= 11:
                    if k == 8:
                        dve.wait_ge(xc_ready, 1)
                    part = conv_out[:, 4 * (k - 8):4 * (k - 8) + 4]
                    nc.vector.tensor_tensor(part, part, across, ALU.add).then_inc(xc_ready, 1)
                if k == 18:
                    dve.wait_ge(var_ps, 1)
                    dve.wait_ge(xc_ready, 5)
                    nc.vector.tensor_scalar(ln_stat[:], X[0][:, 0:T], 1.0 / CW, EPS, ALU.mult, ALU.add).then_inc(var_ready, 1)
                if k == 21:
                    dve.wait_ge(deviation_ready, 1)
                    then(nc.vector.reciprocal(ln_stat[:], ln_stat[:]))
                if 22 <= k <= 25:
                    n = k - 22
                    dve.wait_ge(sqc_ready, n + 1)
                    part = conv_out[:, 4 * n:4 * n + 4]
                    nc.vector.tensor_tensor(part, part, across, ALU.mult).then_inc(norm_ready, 1)
            empty_group(GROUP_B + PAIRS - 1, TILE_B + PAIRS * KT, keep_pair)

            def y_low(r, bank, high_ready, ready, tile):
                dve.wait_ge(high_ready, r + 1)
                two = slice(tile, tile + 2)
                nc.vector.tensor_tensor(act_lo[:, two].rearrange("p c t -> p (c t)"), bank[:],
                                        act_hi[:, two].bitcast(F32).rearrange("p c t -> p (c t)"),
                                        ALU.subtract).then_inc(ready, 1)

            s = gates_done = 0
            dve.wait_ge(gate_zeroed, 2)
            for n, kind in enumerate(P_ITEMS):
                if kind == "a":
                    gate_item(gate_sum, 2 * gates_done, n % SLOTS, landed(ITEM_P + n) + EXTRA, 2 * GATE_ITEMS + gates_done)
                    gates_done += 1
                    continue
                for kk in range(2):
                    if s % PKT:
                        low(TILE_P + s, s, n % SLOTS, kk)
                    for r in (s,) if s < 2 else (s - 1,) if 3 <= s < 1 + CT // 2 else ():
                        dve.wait_ge(conv_hi, r + 1)
                        two = slice(2 * r, 2 * r + 2)
                        nc.vector.tensor_tensor(act_lo[:, two], conv_out[:, two], act_hi[:, two].bitcast(F32),
                                                ALU.subtract).then_inc(conv_lo, 1)
                    attend_at(s, PAIRS - 1)
                    if s - 3 in SB_ROUNDS:
                        r = SB_ROUNDS.index(s - 3)
                        y_low(r, X[0], ysb_hi, ysb_lo, KT // 2 + 2 * r)
                    if s % PKT == PKT - 1:
                        gates = gatebuf[:, s // PKT]
                        empty_group(GROUP_P + s // PKT, TILE_P + s + 1, lambda bank, t, columns: nc.vector.tensor_tensor(
                            gates[:, t, columns], gates[:, t, columns], bank, ALU.mult), (n + 1) % SLOTS)
                    s += 1

            def out_group(g, kinds, item, gates, done, after):
                k = a_items = 0
                for n, kind in enumerate(kinds):
                    if kind == "a":
                        gate_item(gate_sum, gates + 2 * a_items, n % SLOTS, item(n), done + a_items)
                        a_items += 1
                        continue
                    for kk in range(2):
                        if k:
                            low(TILE_O + g * KT + k, k, n % SLOTS, kk)
                        after(k)
                        if k == KT - 4:
                            dve.wait_ge(gate_ps, ONE + g)
                            nc.vector.tensor_tensor(gate_diag, ident[:].unsqueeze(1).to_broadcast([P, GC // P, P]),
                                                    gate_cols[:, g].unsqueeze(2).to_broadcast([P, GC // P, P]),
                                                    ALU.mult).then_inc(diag_ready, 1)
                        k += 1
                dve.wait_ge(gate_ready, ONE + 2 * g + 2)
                dve.wait_ge(y_out_free, ONE + g)
                empty_group(GROUP_O + g, TILE_O + g * KT + KT, lambda bank, t, columns: nc.vector.tensor_tensor(
                    y_out[:, t, columns], bank, gate_sb[:, columns], ALU.mult), None if isinstance(g, int) and g == OG - 1 else 0)

            def add_x(g):
                dve.wait_ge(xres_landed, 16 * g + 16)
                dve.wait_ge(bank_free, 4 * (GROUP_O + g + 1) + 4)
                for t in range(TT):
                    nc.vector.tensor_tensor(y_out[:, t], y_out[:, t], x_res[:, t], ALU.add).then_inc(out_ready, 1)

            def first_group(k):
                if k - 3 in LATE_ROUNDS:
                    n = LATE_ROUNDS.index(k - 3)
                    if n == 0:
                        y_low(CT // 2 - 1, X[0], ysb_hi, ysb_lo, KT - 2)
                    else:
                        y_low(n - 1, X[n % 2], yc_hi, yc_lo, 2 * (n - 1))
                if k == KT - 4:
                    dve.wait_ge(gcol_ready, 2)
                if k == KT - 2:
                    gate_column(2, X[0])

            def next_group(g, k):
                if k == 3:
                    add_x(g - 1)

            def last_group(k):
                next_group(OG - 1, k)
                if k == 4:
                    gate_column(3, X[0])
                if k == KT - 4:
                    dve.wait_ge(gcol_ready, OG)

            out_group(0, O_BODY, lambda n: landed(ITEM_O + n) + EXTRA, GATE_ITEMS, 2 * GATE_ITEMS + GATE_ITEMS // 2, first_group)
            dve.wait_ge(gate_zeroed, 3)
            dve.wait_ge(gcol_ready, 3)
            with dve.Fori(1, OG - 1) as g:
                out_group(g, O_BODY, lambda n: landed(ITEM_O1 + n) + EXTRA + (g - 1) * (len(O_BODY) // SLOTS * 16),
                          (g - 1) * GATE_ITEMS, 3 * GATE_ITEMS + (g - 1) * (GATE_ITEMS // 2), lambda k: next_group(g, k))
            out_group(OG - 1, O_LAST, lambda n: landed(ITEM_O3 + n) + EXTRA, 0, 4 * GATE_ITEMS, last_group)
            add_x(OG - 1)


_INS = ["x", "c", "norm_g", "w_ada", "b_ada", "w_in", "q_norm_g", "k_norm_g", "w_dw", "b_dw", "ln_g", "ln_b",
        "w_pw", "b_pw", "w_out"]


def kernel(**inputs):
    import concourse.bacc as bacc
    from concourse.bass_utils import run_bass_kernel_spmd

    nc = bacc.Bacc("TRN2", target_bir_lowering=False, num_devices=1)
    arrays, args = {}, []
    for name in _INS:
        a = np.ascontiguousarray(inputs[name])
        arrays[f"in_{name}"] = a
        args.append(nc.dram_tensor(f"in_{name}", a.shape, mybir.dt.from_np(a.dtype), kind="ExternalInput").ap())
    out = nc.dram_tensor("out_x", (1, T, D), F32, kind="ExternalOutput").ap()
    hybrid_layer(nc, *args, out)
    r = run_bass_kernel_spmd(nc, [arrays], core_ids=[0])
    return r.results[0]["out_x"]
```
